# Optimizing a Trainium2 kernel written in Bass

```python
import jax, jax.numpy as jnp
from jax import lax
import numpy as np

D_MODEL = 1024
BATCH = 1
SEQ = 256
DEPTH = 2

N_MIXERS = 2
A_HEADS = 8
A_HEAD_DIM = D_MODEL // A_HEADS
MOBA_BLOCK = 256
MOBA_TOPK = 3
MOBA_QCHUNK = 64
R_HEADS = 4
R_QK_DIM = D_MODEL // R_HEADS
R_V_DIM = 2 * D_MODEL // R_HEADS
R_CHUNK = 128
D_FF = 4 * D_MODEL
ROPE_THETA = 10000.0
EPS = 1e-6
NEG = -1e30
N_A = (DEPTH + 1) // 2
N_R = DEPTH // 2

kernel_name = "moba_retention_hybrid_trunk"

def rms_norm(x, g):
    xf = x.astype(jnp.float32)
    y = xf * lax.rsqrt(jnp.mean(xf * xf, axis=-1, keepdims=True) + EPS)
    return (y * g.astype(jnp.float32)).astype(x.dtype)

def rope(x, pos):
    half = x.shape[-1] // 2
    inv = ROPE_THETA ** (-jnp.arange(half, dtype=jnp.float32) / half)
    ang = pos.astype(jnp.float32)[:, None] * inv[None, :]
    cos = jnp.cos(ang)[:, None, :]
    sin = jnp.sin(ang)[:, None, :]
    xf = x.astype(jnp.float32)
    x1, x2 = xf[..., :half], xf[..., half:]
    return jnp.concatenate([x1 * cos - x2 * sin, x2 * cos + x1 * sin], axis=-1).astype(x.dtype)

def moba_attention(q, k, v):
    B, H, S, Dh = q.shape
    nb = -(-S // MOBA_BLOCK)
    pad = nb * MOBA_BLOCK - S
    kp = jnp.pad(k, ((0, 0), (0, 0), (0, pad), (0, 0)))
    vp = jnp.pad(v, ((0, 0), (0, 0), (0, pad), (0, 0)))
    kb = kp.reshape(B, H, nb, MOBA_BLOCK, Dh)
    vb = vp.reshape(B, H, nb, MOBA_BLOCK, Dh)
    kmean = jnp.mean(kb.astype(jnp.float32), axis=3)
    ksel = min(MOBA_TOPK, nb)
    scale = Dh ** -0.5
    n_chunks = S // MOBA_QCHUNK
    qc = q.reshape(B, H, n_chunks, MOBA_QCHUNK, Dh).transpose(2, 0, 1, 3, 4)
    bi = jnp.arange(B)[:, None, None]
    hi = jnp.arange(H)[None, :, None]

    def one_chunk(args):
        c, q_c = args
        start = c * MOBA_QCHUNK
        own = start // MOBA_BLOCK
        qpos = start + jnp.arange(MOBA_QCHUNK)
        gate = jnp.einsum('bhqd,bhnd->bhqn', q_c, kmean, preferred_element_type=jnp.float32)
        gate = jnp.where(jnp.arange(nb) < own, gate, NEG)
        _, top_i = lax.top_k(gate, ksel)
        valid = top_i < own
        k_own = lax.dynamic_slice_in_dim(kp, own * MOBA_BLOCK, MOBA_BLOCK, axis=2)
        v_own = lax.dynamic_slice_in_dim(vp, own * MOBA_BLOCK, MOBA_BLOCK, axis=2)
        kpos = own * MOBA_BLOCK + jnp.arange(MOBA_BLOCK)
        s_own = jnp.einsum('bhqd,bhkd->bhqk', q_c, k_own, preferred_element_type=jnp.float32) * scale
        s_own = jnp.where(kpos[None, :] <= qpos[:, None], s_own, NEG)
        scores = [s_own]
        for j in range(ksel):
            k_sel = kb[bi, hi, top_i[..., j]]
            s = jnp.einsum('bhqd,bhqkd->bhqk', q_c, k_sel, preferred_element_type=jnp.float32) * scale
            scores.append(jnp.where(valid[..., j, None], s, NEG))
        p = jax.nn.softmax(jnp.concatenate(scores, axis=-1), axis=-1).astype(v.dtype)
        p_parts = jnp.split(p, 1 + ksel, axis=-1)
        out = jnp.einsum('bhqk,bhkd->bhqd', p_parts[0], v_own)
        for j in range(ksel):
            v_sel = vb[bi, hi, top_i[..., j]]
            out = out + jnp.einsum('bhqk,bhqkd->bhqd', p_parts[j + 1], v_sel)
        return out

    out = lax.map(one_chunk, (jnp.arange(n_chunks), qc))
    return out.transpose(1, 2, 0, 3, 4).reshape(B, H, S, Dh)

def moba_mixer(h, w_qkv, q_gain, k_gain, w_o, pos):
    B, S, _ = h.shape
    q, k, v = jnp.split(h @ w_qkv, 3, axis=-1)
    q = rope(rms_norm(q.reshape(B, S, A_HEADS, A_HEAD_DIM), q_gain), pos)
    k = rope(rms_norm(k.reshape(B, S, A_HEADS, A_HEAD_DIM), k_gain), pos)
    v = v.reshape(B, S, A_HEADS, A_HEAD_DIM)
    o = moba_attention(q.transpose(0, 2, 1, 3), k.transpose(0, 2, 1, 3), v.transpose(0, 2, 1, 3))
    return o.transpose(0, 2, 1, 3).reshape(B, S, D_MODEL) @ w_o

def retention_chunkwise(q, k, v):
    B, H, S, Dk = q.shape
    Dv = v.shape[-1]
    C = R_CHUNK
    nc = S // C
    log_g = jnp.log1p(-(2.0 ** (-5.0 - jnp.arange(H, dtype=jnp.float32))))
    idx = jnp.arange(C, dtype=jnp.float32)
    diff = idx[:, None] - idx[None, :]
    dmat = jnp.where(diff >= 0, jnp.exp(log_g[:, None, None] * jnp.maximum(diff, 0.0)), 0.0)
    xi = jnp.exp(log_g[:, None] * (idx + 1.0))
    zeta = jnp.exp(log_g[:, None] * (C - 1.0 - idx))
    g_chunk = jnp.exp(log_g * C)
    qc = q.astype(jnp.float32).reshape(B, H, nc, C, Dk)
    kc = k.astype(jnp.float32).reshape(B, H, nc, C, Dk)
    vc = v.astype(jnp.float32).reshape(B, H, nc, C, Dv)
    s = jnp.einsum('bhnqd,bhnkd->bhnqk', qc, kc) * dmat[None, :, None]
    inner = jnp.einsum('bhnqk,bhnkd->bhnqd', s, vc)

    def step(R, inp):
        q_i, k_i, v_i = inp
        cross = jnp.einsum('bhqd,bhde->bhqe', q_i, R) * xi[None, :, :, None]
        R = R * g_chunk[None, :, None, None] + jnp.einsum('bhkd,bhke->bhde', k_i * zeta[None, :, :, None], v_i)
        return R, cross

    R0 = jnp.zeros((B, H, Dk, Dv), jnp.float32)
    _, cross = lax.scan(step, R0, (jnp.moveaxis(qc, 2, 0), jnp.moveaxis(kc, 2, 0), jnp.moveaxis(vc, 2, 0)))
    out = inner + cross.transpose(1, 2, 0, 3, 4)
    return out.reshape(B, H, S, Dv)

def retention_mixer(h, w_in, w_out, pos):
    B, S, _ = h.shape
    q, k, v, g = jnp.split(h @ w_in, [D_MODEL, 2 * D_MODEL, 4 * D_MODEL], axis=-1)
    q = rope(q.reshape(B, S, R_HEADS, R_QK_DIM), pos)
    k = rope(k.reshape(B, S, R_HEADS, R_QK_DIM), pos) * (R_QK_DIM ** -0.5)
    v = v.reshape(B, S, R_HEADS, R_V_DIM)
    y = retention_chunkwise(q.transpose(0, 2, 1, 3), k.transpose(0, 2, 1, 3), v.transpose(0, 2, 1, 3))
    y = y * lax.rsqrt(jnp.mean(y * y, axis=-1, keepdims=True) + EPS)
    y = y.transpose(0, 2, 1, 3).reshape(B, S, 2 * D_MODEL).astype(h.dtype)
    return (jax.nn.silu(g) * y) @ w_out

def sqrelu_mlp(h, w1, w2):
    return jnp.square(jax.nn.relu(h @ w1)) @ w2

def setup_inputs(seed: int = 0) -> dict:
    key = jax.random.key(seed)
    ks = jax.random.split(key, 12)
    f32 = jnp.float32
    D = D_MODEL
    return {
        "x": jax.random.normal(ks[0], (BATCH, SEQ, D), f32),
        "norm_mix_g": 1.0 + 0.05 * jax.random.normal(ks[1], (DEPTH, D), f32),
        "norm_mlp_g": 1.0 + 0.05 * jax.random.normal(ks[2], (DEPTH, D), f32),
        "a_w_qkv": jax.random.normal(ks[3], (N_A, D, 3 * D), f32) * D ** -0.5,
        "a_q_gain": 1.0 + 0.05 * jax.random.normal(ks[4], (N_A, A_HEAD_DIM), f32),
        "a_k_gain": 1.0 + 0.05 * jax.random.normal(ks[5], (N_A, A_HEAD_DIM), f32),
        "a_w_o": jax.random.normal(ks[6], (N_A, D, D), f32) * D ** -0.5,
        "r_w_in": jax.random.normal(ks[7], (N_R, D, 6 * D), f32) * D ** -0.5,
        "r_w_out": jax.random.normal(ks[8], (N_R, 2 * D, D), f32) * (2 * D) ** -0.5,
        "mlp_w1": jax.random.normal(ks[9], (DEPTH, D, D_FF), f32) * D ** -0.5,
        "mlp_w2": jax.random.normal(ks[10], (DEPTH, D_FF, D), f32) * D_FF ** -0.5,
    }

def reference(x, norm_mix_g, norm_mlp_g, a_w_qkv, a_q_gain, a_k_gain, a_w_o, r_w_in, r_w_out, mlp_w1, mlp_w2):
    pos = jnp.arange(x.shape[1], dtype=jnp.int32)
    for i in range(DEPTH):
        h = rms_norm(x, norm_mix_g[i])
        if i % N_MIXERS == 0:
            j = i // N_MIXERS
            x = x + moba_mixer(h, a_w_qkv[j], a_q_gain[j], a_k_gain[j], a_w_o[j], pos)
        else:
            j = i // N_MIXERS
            x = x + retention_mixer(h, r_w_in[j], r_w_out[j], pos)
        x = x + sqrelu_mlp(rms_norm(x, norm_mlp_g[i]), mlp_w1[i], mlp_w2[i])
    return x


_drawn_inputs = setup_inputs


def setup_inputs(seed=0):
    import zlib

    import numpy as np

    out = dict(_drawn_inputs(seed))
    spreads = {}
    factors = {'a_q_gain': 4.726, 'a_k_gain': 4.112}
    for name, (base, spread) in spreads.items():
        noise = np.random.default_rng([zlib.crc32(name.encode()), seed]).standard_normal(out[name].shape)
        drawn = base * np.exp(spread * noise) if base else spread * noise
        out[name] = __import__('jax').numpy.asarray(drawn.astype(out[name].dtype))
    for name, factor in factors.items():
        out[name] = (out[name] * factor).astype(out[name].dtype)
    return out
```

```python
from contextlib import ExitStack, contextmanager

import numpy as np

import concourse.bass as bass
from concourse import mybir

F32 = mybir.dt.float32
F32R = mybir.dt.float32r
BF16 = mybir.dt.bfloat16
ACT = mybir.ActivationFunctionType
ALU = mybir.AluOpType
AX = mybir.AxisListType.X

P = 128
SEQ = 256
D = 1024
FF = 4096
TT = SEQ // P
KD = D // P
KF = FF // P
HA = 8
HR = 4
DK = D // HR
DV = 2 * D // HR
THETA = 10000.0
EPS = 1e-6
NEG = -1e30

RING = 4
AHEAD = RING - 1
CH = 2048
NC = 512
MC = 256

C_QKV = 0
C_WO = C_QKV + 12
C_W1 = [C_WO + 4, 80]
C_W2 = [C_W1[0] + 16, 96]
C_QK = C_W2[0] + 16
C_VG = C_QK + 8
C_WOUT = C_VG + 16
CHUNKS = 112
B_QKV = 0
B_WO = 12
B_W1 = [16, 64]
B_W2 = [32, 80]
B_QK = 36
B_VG = 44
B_WOUT = 60


class Ticks:

    def __init__(self, sem):
        self.sem, self.n, self.shift = sem, 0, 0

    def mark(self, instruction):
        instruction.then_inc(self.sem, 1)
        self.n += 1
        return self.n + self.shift

    def now(self):
        return self.n + self.shift


def program(nc, x_in, tables, norm_mix_g, norm_mlp_g, a_w_qkv, a_q_gain, a_k_gain, a_w_o, r_w_in,
            r_w_out, mlp_w1, mlp_w2, out):
    rope_a, rope_r, decay, causal, ident_in = tables
    with ExitStack() as ctx:
        def sb(name, shape, dt=F32):
            return ctx.enter_context(nc.sbuf_tensor(name, shape, dt))

        def sem(name):
            return ctx.enter_context(nc.semaphore(name))

        raw = sb("raw", [P, RING, CH])
        hi = sb("hi", [P, RING, CH], F32R)
        lo = sb("lo", [P, RING, CH], F32R)
        x = sb("x", [P, TT, D])
        hT_hi = sb("hT_hi", [P, KD, SEQ], F32R)
        hT_lo = sb("hT_lo", [P, KD, SEQ], F32R)
        stage_a = sb("stage_a", [P, 2, 512])
        stage_b = sb("stage_b", [P, 2, 512])
        decay_sb = sb("decay_sb", [P, HR, 384])
        rope_r_sb = sb("rope_r_sb", [P, 2, 2, SEQ])
        sT = sb("sT", [P, 384])
        ident = sb("ident", [P, P])
        gcol = sb("gcol", [P, 4, KD])
        junk = sb("junk", [P, 512], BF16)
        ssq = sb("ssq", [P, TT, 2])
        nrm = sb("nrm", [P, 8, TT])
        half = sb("half", [P, 8])
        small = sb("small", [P, 64])
        sb("arena", [P, 2 * KF * SEQ])
        arena_at = nc.sbuf_base - 2 * KF * SEQ * 4

        def at(name, offset, shape, dt=F32):
            return nc.alloc_sbuf_tensor_at(name, shape, dt, offset=arena_at + offset)

        KB = 1024
        aT_hi = at("aT_hi", 0, [P, KF, SEQ], F32R)
        aT_lo = at("aT_lo", 32 * KB, [P, KF, SEQ], F32R)
        qkT = at("qkT", 0, [P, 2, HA, SEQ])
        v_att = at("v_att", 16 * KB, [P, TT, D])
        oT_hi = at("oT_hi", 24 * KB, [P, HA, SEQ], F32R)
        oT_lo = at("oT_lo", 32 * KB, [P, HA, SEQ], F32R)
        q_raw = at("q_raw", 40 * KB, [P, 2, 512])
        rot = at("rot", 44 * KB, [P, 4, 512])
        probs = at("probs", 40 * KB, [P, 3, 384])
        pT = at("pT", 45 * KB, [P, 2, 384])
        rope_t = at("rope_t", 52 * KB, [P, TT, 2, P])
        gains = at("gains", 54 * KB, [P, 2, P])
        rope_g = at("rope_g", 55 * KB, [P, 2, TT, 2, P])
        mask = at("mask", 59 * KB, [P, 384])
        zT_hi = at("zT_hi", 0, [P, 16, SEQ], F32R)
        zT_lo = at("zT_lo", 16 * KB, [P, 16, SEQ], F32R)
        qk_r = at("qk_r", 32 * KB, [P, 8, 2, SEQ])
        v_r = at("v_r", 48 * KB, [P, TT, DV])
        sg = at("sg", 52 * KB, [P, TT, DV])
        k_cur = at("k_cur", 56 * KB, [P, 2, SEQ])

        acc = ctx.enter_context(nc.psum_tensor("acc", [P, 4, 512], F32))
        scr = ctx.enter_context(nc.psum_tensor("scr", [P, 4, 512], F32))

        raw_ready = [sem(f"raw_ready{s}") for s in range(RING)]
        consts_in = sem("consts_in")
        x_in_ready = sem("x_in_ready")
        hi_ready = sem("hi_ready")
        lo_ready = sem("lo_ready")
        used = sem("used")
        tok0_ready = sem("tok0_ready")
        acc_free = sem("acc_free")
        x_ready = sem("x_ready")
        xT_ready = sem("xT_ready")
        hT_hi_ready = sem("hT_hi_ready")
        hT_ready = sem("hT_ready")
        ssq_ready = sem("ssq_ready")
        dv = Ticks(sem("dve_step"))
        pl = Ticks(sem("pool_step"))
        relu_done = sem("relu_done")
        sq_ready = sem("sq_ready")
        aT_ready = sem("aT_ready")
        var_ready = sem("var_ready")
        pow_ready = sem("pow_ready")
        r_ready = sem("r_ready")
        raw_qk = sem("raw_qk")
        u_ready = sem("u_ready")
        rot_ready = sem("rot_ready")
        rotT_ready = sem("rotT_ready")
        qkT_ready = sem("qkT_ready")
        v_ready = sem("v_ready")
        s_ready = sem("s_ready")
        m_ready = sem("m_ready")
        e_ready = sem("e_ready")
        p_ready = sem("p_ready")
        pTp_ready = sem("pTp_ready")
        pT_ready = sem("pT_ready")
        o_ready = sem("o_ready")
        oT_hi_ready = sem("oT_hi_ready")
        oT_ready = sem("oT_ready")
        t_ready = sem("t_ready")
        qk_r_ready = sem("qk_r_ready")
        k_cur_ready = sem("k_cur_ready")
        v_r_ready = sem("v_r_ready")
        sg_ready = sem("sg_ready")
        sr_ready = sem("sr_ready")
        sT_ready = sem("sT_ready")
        y_ready = sem("y_ready")
        yss_ready = sem("yss_ready")
        z_ready = sem("z_ready")
        zTp_ready = sem("zTp_ready")
        zT_hi_ready = sem("zT_hi_ready")
        zT_ready = sem("zT_ready")
        out_done = sem("out_done")

        def token_chunks(w):
            return w.rearrange("(kg kt p) (n c) -> n kg p kt c", kt=4, p=P, c=NC)

        def feature_chunks(w):
            return w.rearrange("(kt p) (m c) -> m p kt c", p=P, c=MC)

        qkv_w, wo_w, wout_w = token_chunks(a_w_qkv[0]), token_chunks(a_w_o[0]), token_chunks(r_w_out[0])
        vg_w, qk_w = token_chunks(r_w_in[0]), feature_chunks(r_w_in[0])
        w1_w = [feature_chunks(mlp_w1[i]) for i in range(2)]
        w2_w = [token_chunks(mlp_w2[i]) for i in range(2)]
        QKV_ORDER = [0, 2, 1, 3, 4, 5]

        def tok_view(ring, s):
            return ring[:, s, :].rearrange("p (kt c) -> p kt c", c=NC)

        def feat_view(ring, s):
            return ring[:, s, :].rearrange("p (kt c) -> p kt c", c=MC)

        block = ctx.enter_context(nc.Block())

        @block.sync
        def _(sp):
            def load(g, s, view, src):
                sp.wait_ge(lo_ready, 4 * g + (s + 1))
                sp.dma_start(view(raw, s), src).then_inc(raw_ready[s], 16)

            def load_w1(layer):
                with sp.Fori(0, 4) as i:
                    for s in range(RING):
                        load(i + C_W1[layer] // 4, s, feat_view, w1_w[layer][i * 4 + s])

            def load_w2(layer):
                with sp.Fori(0, 2) as n:
                    for kg in range(8):
                        load(n * 2 + (C_W2[layer] // 4 + kg // 4), kg % 4, tok_view,
                             w2_w[layer][n, kg])

            xv = x_in[0].rearrange("(t p) d -> p t d", p=P)
            for t in range(TT):
                sp.dma_start(x[:, t, :], xv[:, t, :]).then_inc(x_in_ready, 16)
            for j, n in enumerate(QKV_ORDER):
                for kg in range(2):
                    c = C_QKV + 2 * j + kg
                    load(c // 4, c % 4, tok_view, qkv_w[n, kg])
            for n in range(2):
                for kg in range(2):
                    load(C_WO // 4, 2 * n + kg, tok_view, wo_w[n, kg])
            load_w1(0)
            load_w2(0)
            with sp.Fori(0, 2) as i:
                for s in range(RING):
                    load(i + C_QK // 4, s, feat_view, qk_w[i * 4 + s])
            with sp.Fori(0, HR) as h:
                for s in range(RING):
                    load(h + C_VG // 4, s, tok_view, vg_w[h + (4 if s < 2 else 8), s % 2])
            with sp.Fori(0, 2) as n:
                for kg in range(4):
                    load(n + C_WOUT // 4, kg, tok_view, wout_w[n, kg])
            load_w1(1)
            load_w2(1)
            ov = out[0].rearrange("(t p) d -> p t d", p=P)
            for n in range(2):
                for t in range(TT):
                    sp.wait_ge(x_ready, 4 * 3 + 2 * n + t + 1)
                    sp.dma_start(ov[:, t, n * NC:(n + 1) * NC],
                                 x[:, t, n * NC:(n + 1) * NC]).then_inc(out_done, 16)
            sp.wait_ge(out_done, 16 * 4)

        @block.gpsimd
        def _(pool):
            pool.sem_inc(sq_ready, 2)
            pool.sem_inc(qk_r_ready, 4)
            pool.dma_start(ident[:], ident_in).then_inc(consts_in, 16)
            for i, g in enumerate((norm_mix_g[0], norm_mlp_g[0], norm_mix_g[1], norm_mlp_g[1])):
                with nc.allow_non_contiguous_dma("1024 gains"):
                    pool.dma_start(gcol[:, i, :], g.rearrange("(kt p) -> p kt", p=P)).then_inc(consts_in, 16)
            pool.dma_start(rope_t[:], rope_a).then_inc(consts_in, 16)
            for i, g in enumerate((a_q_gain, a_k_gain)):
                pool.dma_start(gains[:, i, :], g.broadcast_to([P, P])).then_inc(consts_in, 16)
            pool.dma_start(mask[:], causal).then_inc(consts_in, 16)
            pool.dma_start(rope_r_sb[:], rope_r).then_inc(consts_in, 16)
            pool.dma_start(decay_sb[:], decay).then_inc(consts_in, 16)
            half_set = pl.mark(nc.gpsimd.memset(half[:], -0.5))
            pool.wait_ge(pl.sem, half_set)
            pool.wait_ge(consts_in, 16 * 11)
            for i in range(2):
                for t in range(TT):
                    for part in range(2):
                        pl.mark(nc.gpsimd.tensor_tensor(rope_g[:, i, t, part, :], rope_t[:, t, part, :],
                                                        gains[:, i, :], ALU.mult))

            npow = 0

            def power(dst, src, n):
                nonlocal npow
                npow += 1
                pool.wait_ge(var_ready, npow)
                nc.gpsimd.tensor_tensor(dst, src, half[:, 0:n], ALU.pow).then_inc(pow_ready, 1)

            def norm_power():
                power(nrm[:, 1, :], nrm[:, 0, :], TT)

            norm_power()
            pool.wait_ge(pl.sem, pl.now())
            for j in range(4):
                for t in range(TT):
                    p_i = 2 * j + t
                    pool.wait_ge(raw_qk, 2 * p_i + 1)
                    if p_i >= 2:
                        pool.wait_ge(rot_ready, p_i - 1)
                    sin = rope_g[:, j % 2, t, 1, :].unsqueeze(1).broadcast_to([P, 4, P])
                    nc.gpsimd.tensor_tensor(stage_b[:, p_i % 2, :].rearrange("p (h d) -> p h d", d=P),
                                            q_raw[:, p_i % 2, :].rearrange("p (h d) -> p h d", d=P),
                                            sin, ALU.mult).then_inc(u_ready, 1)
                    power(small[:, 8 + 4 * (p_i % 2):12 + 4 * (p_i % 2)],
                          small[:, 4 * (p_i % 2):4 * (p_i % 2) + 4], 4)

            def mlp(layer):
                norm_power()
                with pool.Fori(0, 4) as i:
                    for s in range(4):
                        c = i * 4 + (16 * layer + s)
                        pool.wait_ge(relu_done, c + 1)
                        pool.wait_ge(aT_ready, c + 1)
                        nc.gpsimd.tensor_tensor(stage_b[:, s % 2, :], stage_a[:, s % 2, :],
                                                stage_a[:, s % 2, :], ALU.mult).then_inc(sq_ready, 1)

            mlp(0)
            norm_power()
            with pool.Fori(0, 2) as i:
                for s in range(4):
                    pool.wait_ge(t_ready, i * 4 + (s + 1))
                    a = stage_a[:, s % 2, :].rearrange("p (two t) -> p two t", two=2)
                    b = stage_b[:, s % 2, :].rearrange("p (two t) -> p two t", two=2)
                    for o in range(2):
                        nc.gpsimd.tensor_tensor(qk_r[:, bass.ds(i * 4 + s, 1), o, :], a[:, o:o + 1, :],
                                                b[:, 1 - o:2 - o, :], ALU.add).then_inc(qk_r_ready, 1)
            for h in range(HR):
                power(small[:, 20:22], small[:, 18:20], TT)
            mlp(1)

        @block.tensor
        def _(pe):
            pe.sem_inc(used, RING)

            def chunk_in(g, s):
                pe.wait_ge(lo_ready, 4 * g + (s + 1 + RING))

            def three(dst, a_hi, a_lo, b_hi, b_lo, first, last):
                nc.tensor.matmul(dst, a_hi, b_hi, start=first, stop=False)
                nc.tensor.matmul(dst, a_hi, b_lo, start=False, stop=False)
                return nc.tensor.matmul(dst, a_lo, b_hi, start=False, stop=last)

            def token_form(g0, s0, n_chunks, bank0, bank_slot, lhs, before=lambda kg: None,
                           between=lambda kg: None):
                for kg in range(n_chunks):
                    s = (s0 + kg) % RING
                    before(kg)
                    chunk_in(g0 + (s0 + kg) // RING, s)
                    for t in range(TT):
                        if kg == 0:
                            pe.wait_ge(acc_free, bank0 + (t + 1))
                        for kt in range(4):
                            k = 4 * kg + kt
                            m = three(acc[:, bank_slot + t, :],
                                      lhs[0][:, k, t * P:(t + 1) * P], lhs[1][:, k, t * P:(t + 1) * P],
                                      tok_view(hi, s)[:, kt, :], tok_view(lo, s)[:, kt, :],
                                      k == 0, k == 4 * n_chunks - 1)
                        if t == 0 and kg == n_chunks - 1:
                            m.then_inc(tok0_ready, 1)
                    m.then_inc(used, 1)
                    between(kg)

            def feature_form(g, s, bank0, hT_need=None):
                chunk_in(g, s)
                pe.wait_ge(acc_free, bank0 + 1)
                for o in range(2):
                    for kt in range(KD):
                        if hT_need is not None and o == 0:
                            pe.wait_ge(hT_ready, hT_need + kt + 1)
                        m = three(acc[:, s, o * SEQ:(o + 1) * SEQ],
                                  feat_view(hi, s)[:, kt, o * P:(o + 1) * P],
                                  feat_view(lo, s)[:, kt, o * P:(o + 1) * P],
                                  hT_hi[:, kt, :], hT_lo[:, kt, :], kt == 0, kt == KD - 1)
                m.then_inc(used, 1)

            def transpose_x(norm, kts):
                for kt in kts:
                    pe.wait_ge(hT_ready, 8 * norm + kt + 1)
                    for t in range(TT):
                        if norm > 0:
                            pe.wait_ge(x_ready, 4 * (norm - 1) + 2 * (kt // 4) + t + 1)
                        m = nc.tensor.transpose(scr[:, kt % 4, t * P:(t + 1) * P],
                                                x[:, t, kt * P:(kt + 1) * P], ident[:])
                    m.then_inc(xT_ready, 1)

            def early_x(norm):
                return lambda kg: transpose_x(norm, range(4)) if kg == 0 else None

            hT = (hT_hi, hT_lo)
            pe.wait_ge(consts_in, 16 * 11)
            pe.wait_ge(x_in_ready, 16 * TT)
            transpose_x(0, range(KD))

            def transpose_rot(j):
                for t in range(TT):
                    p_i = 2 * j + t
                    pe.wait_ge(rot_ready, p_i + 1)
                    pe.wait_ge(qkT_ready, max(p_i - 3, 0)) if p_i >= 4 else None
                    for h in range(4):
                        m = nc.tensor.transpose(scr[:, p_i % 4, h * P:(h + 1) * P],
                                                rot[:, p_i % 4, h * P:(h + 1) * P], ident[:])
                    m.then_inc(rotT_ready, 1)

            pe.wait_ge(hT_ready, 4 + 8)
            for j in range(6):
                token_form((C_QKV + 2 * j) // 4, 2 * j % 4, 2, B_QKV + 2 * j, 2 * j % 4, hT)
                if 1 <= j <= 4:
                    transpose_rot(j - 1)

            def scores(h):
                if h == 0:
                    pe.wait_ge(qkT_ready, 8)
                if h >= 2:
                    pe.wait_ge(m_ready, h - 1)
                nc.tensor.matmul(scr[:, h % 2, 0:P], qkT[:, 0, h, 0:P], qkT[:, 1, h, 0:P],
                                 start=True, stop=True)
                nc.tensor.matmul(scr[:, h % 2, P:384], qkT[:, 0, h, P:SEQ], qkT[:, 1, h, :],
                                 start=True, stop=True).then_inc(s_ready, 1)

            def transpose_p(h):
                pe.wait_ge(p_ready, h + 1)
                if h >= 1:
                    pe.wait_ge(pT_ready, h)
                b = scr[:, 2, :]
                p = probs[:, h % 3, :]
                nc.tensor.transpose(b[:, 0:P], p[:, 0:P], ident[:])
                nc.tensor.transpose(b[:, P:2 * P], p[:, P:2 * P], ident[:])
                nc.tensor.transpose(b[:, 2 * P:384], p[:, 2 * P:384], ident[:]).then_inc(pTp_ready, 1)

            def attend(h):
                if h == 0:
                    pe.wait_ge(v_ready, 4)
                pe.wait_ge(pT_ready, h + 1)
                if h >= 1:
                    pe.wait_ge(oT_ready, h)
                nc.tensor.matmul(scr[:, 3, 0:SEQ], v_att[:, 0, h * P:(h + 1) * P], pT[:, h % 2, 0:SEQ],
                                 start=True, stop=False)
                nc.tensor.matmul(scr[:, 3, P:SEQ], v_att[:, 1, h * P:(h + 1) * P],
                                 pT[:, h % 2, SEQ:384], start=False, stop=True).then_inc(o_ready, 1)

            for h in range(HA + 3):
                if h < HA:
                    scores(h)
                if 2 <= h < HA + 2:
                    transpose_p(h - 2)
                if h >= 3:
                    attend(h - 3)

            for n in range(2):
                token_form(C_WO // 4, 2 * n, 2, B_WO + 2 * n, 2 * n, (oT_hi, oT_lo),
                           before=lambda kg: pe.wait_ge(oT_ready, 4 * kg + 4),
                           between=early_x(1) if n == 1 else (lambda kg: None))
            transpose_x(1, range(4, KD))

            def mlp(layer, norm):
                feature_form(C_W1[layer] // 4, 0, B_W1[layer], hT_need=4 + 8 * norm)
                for s in range(1, 4):
                    feature_form(C_W1[layer] // 4, s, B_W1[layer] + s)
                with pe.Fori(1, 4) as i:
                    for s in range(4):
                        feature_form(i + C_W1[layer] // 4, s, i * 4 + (B_W1[layer] + s))
                for n in range(2):
                    token_form(C_W2[layer] // 4 + 2 * n, 0, 8, B_W2[layer] + 2 * n, 2 * n,
                               (aT_hi, aT_lo),
                               before=(lambda kg: pe.wait_ge(aT_ready, 2 + 16 * layer + 2 * kg + 2))
                               if n == 0 else (lambda kg: None),
                               between=early_x(norm + 1) if n == 1 and layer == 0 else (lambda kg: None))

            mlp(0, 1)
            transpose_x(2, range(4, KD))

            feature_form(C_QK // 4, 0, B_QK, hT_need=4 + 8 * 2)
            for s in range(1, 4):
                feature_form(C_QK // 4, s, B_QK + s)
            for s in range(4):
                feature_form(C_QK // 4 + 1, s, B_QK + 4 + s)

            def z_transposes(h):
                for t in range(TT):
                    pe.wait_ge(z_ready, h * 2 + (t + 1))
                    pe.wait_ge(zT_ready, h * 2 + (t + 1))
                    for a in range(4):
                        m = nc.tensor.transpose(scr[:, 3, a * P:(a + 1) * P],
                                                sg[:, t, a * P:(a + 1) * P], ident[:])
                    m.then_inc(zTp_ready, 1)

            def head(h, first):
                token_form(h + C_VG // 4, 0, 2, h * 4 + B_VG, 0, hT)
                pe.wait_ge(k_cur_ready, h + 1)
                if not first:
                    pe.wait_ge(sT_ready, h)
                for half_d in range(2):
                    nc.tensor.matmul(scr[:, 0, 0:SEQ], k_cur[:, half_d, 0:P],
                                     qk_r[:, bass.ds(h, 1), half_d, :].rearrange("p a t -> p (a t)"),
                                     start=half_d == 0, stop=half_d == 1)
                for half_d in range(2):
                    m = nc.tensor.matmul(scr[:, 0, SEQ:384], k_cur[:, half_d, P:SEQ],
                                         qk_r[:, bass.ds(h, 1), half_d, P:SEQ].rearrange("p a t -> p (a t)"),
                                         start=half_d == 0, stop=half_d == 1)
                m.then_inc(sr_ready, 1)
                if not first:
                    z_transposes(h - 1)
                token_form(h + C_VG // 4, 2, 2, h * 4 + (B_VG + 2), 2, hT)
                pe.wait_ge(sT_ready, h + 1)
                pe.wait_ge(v_r_ready, h * 2 + 2)
                nc.tensor.matmul(scr[:, 1, :], sT[:, 0:P], v_r[:, 0, :],
                                 start=True, stop=True).then_inc(y_ready, 1)
                nc.tensor.matmul(scr[:, 2, :], sT[:, P:SEQ], v_r[:, 0, :], start=True, stop=False)
                nc.tensor.matmul(scr[:, 2, :], sT[:, SEQ:384], v_r[:, 1, :],
                                 start=False, stop=True).then_inc(y_ready, 1)

            head(0, True)
            with pe.Fori(1, HR) as h:
                head(h, False)
            z_transposes(HR - 1)

            for n in range(2):
                token_form(C_WOUT // 4 + n, 0, 4, B_WOUT + 2 * n, 2 * n, (zT_hi, zT_lo),
                           before=lambda kg: pe.wait_ge(zT_ready, 1 + 2 * (kg + 1)),
                           between=early_x(3) if n == 1 else (lambda kg: None))
            transpose_x(3, range(4, KD))
            mlp(1, 3)

        @block.scalar
        def _(act):
            def split(g, s):
                act.wait_ge(raw_ready[s], g * 16 + 16)
                act.wait_ge(used, 4 * g + (s + 1))
                nc.scalar.activation(hi[:, s, :], raw[:, s, :], ACT.Copy).then_inc(hi_ready, 1)

            def split_ahead(g, s):
                split(g + (s + AHEAD) // RING, (s + AHEAD) % RING)

            def norm_hi(norm, kts):
                for kt in kts:
                    act.wait_ge(xT_ready, 8 * norm + kt + 1)
                    nc.scalar.activation(hT_hi[:, kt, :], scr[:, kt % 4, 0:SEQ], ACT.Copy,
                                         scale=gcol[:, norm, kt:kt + 1]).then_inc(hT_hi_ready, 1)

            def norm_squares(norm):
                for t in range(TT):
                    for n in range(2):
                        if norm + t + n > 0:
                            act.wait_ge(ssq_ready, 4 * norm + 2 * t + n)
                        nc.scalar.activation(junk[:], x[:, t, n * NC:(n + 1) * NC], ACT.Square,
                                             accum_out=ssq[:, t, n:n + 1]).then_inc(ssq_ready, 1)

            act.wait_ge(consts_in, 16 * 11)
            act.wait_ge(x_in_ready, 16 * TT)
            norm_hi(0, range(KD))
            norm_squares(0)
            for s in range(AHEAD):
                split(0, s)

            def store_qkT(j):
                for t in range(TT):
                    p_i = 2 * j + t
                    act.wait_ge(rotT_ready, p_i + 1)
                    nc.scalar.copy(qkT[:, j % 2, 4 * (j // 2):4 * (j // 2) + 4, t * P:(t + 1) * P],
                                   scr[:, p_i % 4, :].rearrange("p (h t) -> p h t", t=P)
                                   ).then_inc(qkT_ready, 1)

            def product_wait(c_last, t, n_tok):
                if t == 0:
                    act.wait_ge(tok0_ready, n_tok + 1)
                else:
                    act.wait_ge(used, c_last + 1 + RING)

            for j in range(6):
                for s in range(2):
                    c = C_QKV + 2 * j + s
                    split_ahead(c // 4, c % 4)
                if 2 <= j <= 5:
                    store_qkT(j - 2)
                for t in range(TT):
                    product_wait(C_QKV + 2 * j + 1, t, j)
                    bank = acc[:, (2 * j + t) % 4, :]
                    if j < 4:
                        p_i = 2 * j + t
                        if p_i >= 2:
                            act.wait_ge(rot_ready, p_i - 1)
                        nc.scalar.copy(q_raw[:, p_i % 2, :], bank).then_inc(raw_qk, 1)
                        nc.scalar.activation(stage_a[:, p_i % 2, :], bank, ACT.Square).then_inc(raw_qk, 1)
                    else:
                        act.wait_ge(r_ready, 1)
                        nc.scalar.activation(v_att[:, t, (j - 4) * 512:(j - 3) * 512], bank, ACT.Copy,
                                             scale=nrm[:, 1, t:t + 1]).then_inc(v_ready, 1)

            def exponentials(h):
                act.wait_ge(m_ready, h + 1)
                for t, (a, b) in enumerate(((0, P), (P, 384))):
                    nc.scalar.activation(probs[:, h % 3, a:b], probs[:, h % 3, a:b], ACT.Exp,
                                         bias=small[:, 48 + 2 * (h % 4) + t:49 + 2 * (h % 4) + t],
                                         scale=small[:, 24 + 8 * t + h:25 + 8 * t + h],
                                         accum_out=small[:, 56 + 2 * (h % 4) + t:57 + 2 * (h % 4) + t]
                                         ).then_inc(e_ready, 1)

            def store_pT(h):
                act.wait_ge(pTp_ready, h + 1)
                if h >= 2:
                    act.wait_ge(o_ready, h - 1)
                nc.scalar.copy(pT[:, h % 2, :], scr[:, 2, 0:384]).then_inc(pT_ready, 1)

            def head_hi(h):
                act.wait_ge(o_ready, h + 1)
                nc.scalar.activation(oT_hi[:, h, :], scr[:, 3, 0:SEQ], ACT.Copy).then_inc(oT_hi_ready, 1)

            for h in range(HA + 3):
                if h < HA:
                    exponentials(h)
                if 2 <= h < HA + 2:
                    store_pT(h - 2)
                if h >= 3:
                    head_hi(h - 3)

            for c in range(4):
                split_ahead(C_WO // 4, c)
                if c == 2:
                    norm_hi(1, range(4))
            norm_hi(1, range(4, KD))

            def mlp(layer, norm):
                act.wait_ge(x_ready, 4 * norm)
                norm_squares(norm)
                with act.Fori(0, 4) as i:
                    for s in range(4):
                        g = i + C_W1[layer] // 4
                        split_ahead(g, s)
                        act.wait_ge(used, g * 4 + (s + 1 + RING))
                        act.wait_ge(sq_ready, i * 4 + (16 * layer + s + 1))
                        nc.scalar.activation(stage_a[:, s % 2, :], acc[:, s, :],
                                             ACT.Relu).then_inc(relu_done, 1)
                for n in range(2):
                    for kg in range(8):
                        if layer == 0 or n == 0 or kg < 8 - AHEAD:
                            split_ahead(C_W2[layer] // 4 + 2 * n + kg // 4, kg % 4)
                        if layer == 0 and n == 1 and kg == 2:
                            norm_hi(norm + 1, range(4))

            mlp(0, 1)
            norm_hi(2, range(4, KD))
            act.wait_ge(x_ready, 8)
            norm_squares(2)
            for c in range(8):
                split_ahead(C_QK // 4 + c // 4, c % 4)

            def store_zT(h):
                for t in range(TT):
                    act.wait_ge(zTp_ready, h * 2 + (t + 1))
                    nc.scalar.activation(zT_hi[:, bass.ds(h * 4, 4), t * P:(t + 1) * P],
                                         scr[:, 3, :].rearrange("p (a t) -> p a t", t=P),
                                         ACT.Copy).then_inc(zT_hi_ready, 1)

            def head(h, first):
                act.wait_ge(qk_r_ready, h * 2 + 14)
                if not first:
                    act.wait_ge(sr_ready, h)
                nc.scalar.copy(k_cur[:], qk_r[:, bass.ds(h + 4, 1), :, :].rearrange("p a b t -> p (a b) t")
                               ).then_inc(k_cur_ready, 1)
                for s in range(2):
                    split_ahead(h + C_VG // 4, s)
                for t in range(TT):
                    if t == 0:
                        act.wait_ge(tok0_ready, h * 2 + (TOK_VG + 1))
                    else:
                        act.wait_ge(used, h * 4 + (C_VG + 2 + RING))
                    if not first:
                        act.wait_ge(y_ready, h * 2)
                    nc.scalar.activation(v_r[:, t, :], acc[:, t, :], ACT.Copy,
                                         scale=nrm[:, 2, t:t + 1]).then_inc(v_r_ready, 1)
                if not first:
                    store_zT(h - 1)
                for s in range(2, 4):
                    split_ahead(h + C_VG // 4, s)
                for t in range(TT):
                    if t == 0:
                        act.wait_ge(tok0_ready, h * 2 + (TOK_VG + 2))
                    else:
                        act.wait_ge(used, h * 4 + (C_VG + 4 + RING))
                    nc.scalar.activation(sg[:, t, :], acc[:, 2 + t, :], ACT.Silu,
                                         scale=nrm[:, 1, t:t + 1]).then_inc(sg_ready, 1)
                for t in range(TT):
                    act.wait_ge(y_ready, h * 2 + (t + 1))
                    if t == 1:
                        act.wait_ge(yss_ready, h * 2 + 1)
                    elif not first:
                        act.wait_ge(z_ready, h * 2)
                    nc.scalar.activation(junk[:], scr[:, 1 + t, :], ACT.Square,
                                         accum_out=small[:, 16 + t:17 + t]).then_inc(yss_ready, 1)

            act.wait_ge(r_ready, 3)
            head(0, True)
            with act.Fori(1, HR) as h:
                head(h, False)
            store_zT(HR - 1)

            for n in range(2):
                for kg in range(4):
                    split_ahead(C_WOUT // 4 + n, kg)
                    if n == 1 and kg == 2:
                        norm_hi(3, range(4))
            norm_hi(3, range(4, KD))
            mlp(1, 3)

        @block.vector
        def _(dve):
            dve.sem_inc(lo_ready, RING)
            dve.sem_inc(hT_ready, 4)
            dve.sem_inc(acc_free, 4)
            dve.sem_inc(aT_ready, 2)
            dve.sem_inc(zT_ready, 1)

            def split(g, s):
                dve.wait_ge(hi_ready, 4 * g + (s + 1))
                nc.vector.tensor_tensor(lo[:, s, :], raw[:, s, :], hi[:, s, :].bitcast(F32),
                                        ALU.subtract).then_inc(lo_ready, 1)

            def split_ahead(g, s):
                split(g + (s + AHEAD) // RING, (s + AHEAD) % RING)

            def norm_lo(norm, kts):
                for kt in kts:
                    dve.wait_ge(hT_hi_ready, 8 * norm + kt + 1)
                    nc.vector.scalar_tensor_tensor(hT_lo[:, kt, :], scr[:, kt % 4, 0:SEQ],
                                                   gcol[:, norm, kt:kt + 1],
                                                   hT_hi[:, kt, :].bitcast(F32), ALU.mult,
                                                   ALU.subtract).then_inc(hT_ready, 1)

            def own(instruction):
                dve.wait_ge(dv.sem, dv.mark(instruction))

            npow = 0

            def power_done():
                nonlocal npow
                npow += 1
                dve.wait_ge(pow_ready, npow)

            def norm_factors(norm):
                dve.wait_ge(ssq_ready, 4 * norm + 4)
                own(nc.vector.tensor_tensor(nrm[:, 0, :], ssq[:, :, 0], ssq[:, :, 1], ALU.add))
                nc.vector.tensor_scalar(nrm[:, 0, :], nrm[:, 0, :], 1.0 / D, EPS, ALU.mult,
                                        ALU.add).then_inc(var_ready, 1)
                power_done()
                own(nc.vector.tensor_tensor(nrm[:, 2, :], nrm[:, 1, :], nrm[:, 1, :], ALU.mult))
                own(nc.vector.tensor_scalar(nrm[:, 3, :], nrm[:, 2, :], 1.0 / P, None, ALU.mult))
                nc.vector.tensor_scalar(nrm[:, 4, :], nrm[:, 2, :], 1.0 / DV, None,
                                        ALU.mult).then_inc(r_ready, 1)
                dve.wait_ge(r_ready, norm + 1)

            norm_lo(0, range(KD))
            norm_factors(0)
            for s in range(AHEAD):
                split(0, s)

            for j in range(6):
                for s in range(2):
                    c = C_QKV + 2 * j + s
                    split_ahead(c // 4, c % 4)
                for t in range(TT):
                    if j >= 4:
                        dve.wait_ge(v_ready, 2 * (j - 4) + t + 1)
                        dve.sem_inc(acc_free, 1)
                        continue
                    p_i = 2 * j + t
                    raw4 = q_raw[:, p_i % 2, :].rearrange("p (h d) -> p h d", d=P)
                    u4 = stage_b[:, p_i % 2, :].rearrange("p (h d) -> p h d", d=P)
                    r4 = rot[:, p_i % 4, :].rearrange("p (h d) -> p h d", d=P)
                    ss = small[:, 4 * (p_i % 2):4 * (p_i % 2) + 4]
                    pw = small[:, 8 + 4 * (p_i % 2):12 + 4 * (p_i % 2)]
                    dve.wait_ge(raw_qk, 2 * p_i + 2)
                    dve.sem_inc(acc_free, 1)
                    own(nc.vector.reduce_sum(ss, stage_a[:, p_i % 2, :].rearrange("p (h d) -> p h d", d=P),
                                             axis=AX))
                    nc.vector.tensor_scalar(ss, ss, nrm[:, 3, t:t + 1], EPS, ALU.mult,
                                            ALU.add).then_inc(var_ready, 1)
                    if p_i >= 4:
                        dve.wait_ge(rotT_ready, p_i - 3)
                    cos = rope_g[:, j % 2, t, 0, :].unsqueeze(1).broadcast_to([P, 4, P])
                    dve.wait_ge(u_ready, p_i + 1)
                    own(nc.vector.tensor_tensor(r4, raw4, cos, ALU.mult))
                    for o in range(2):
                        a, b = slice(o * 64, o * 64 + 64), slice((1 - o) * 64, (1 - o) * 64 + 64)
                        last = nc.vector.tensor_tensor(r4[:, :, a], r4[:, :, a], u4[:, :, b], ALU.add)
                        own(last)
                    power_done()
                    if j % 2 == 0:
                        heads = slice(24 + 8 * t + 4 * (j // 2), 28 + 8 * t + 4 * (j // 2))
                        nc.vector.tensor_scalar(small[:, heads], pw, nrm[:, 1, t:t + 1],
                                                float(P) ** -0.5, ALU.mult,
                                                ALU.mult).then_inc(rot_ready, 1)
                    else:
                        own(nc.vector.tensor_scalar(pw, pw, nrm[:, 1, t:t + 1], None, ALU.mult))
                        nc.vector.tensor_tensor(r4, r4, pw.unsqueeze(2).broadcast_to([P, 4, P]),
                                                ALU.mult).then_inc(rot_ready, 1)

            def masked(h):
                dve.wait_ge(s_ready, h + 1)
                if h == 0:
                    dve.wait_ge(qkT_ready, 8)
                    dve.wait_ge(rot_ready, 8)
                if h >= 3:
                    dve.wait_ge(pTp_ready, h - 2)
                mx = small[:, 40 + 2 * (h % 4):42 + 2 * (h % 4)]
                nc.vector.tensor_tensor(probs[:, h % 3, :], scr[:, h % 2, 0:384], mask[:],
                                        ALU.add).then_inc(dv.sem, 1)
                dv.n += 1
                dve.wait_ge(dv.sem, dv.now())
                nc.vector.reduce_max(mx[:, 0:1], probs[:, h % 3, 0:P], axis=AX).then_inc(dv.sem, 1)
                nc.vector.reduce_max(mx[:, 1:2], probs[:, h % 3, P:384], axis=AX).then_inc(dv.sem, 1)
                dv.n += 2
                dve.wait_ge(dv.sem, dv.now())
                fq = small[:, 24:40].rearrange("p (t h) -> p t h", t=2)[:, :, h]
                nc.vector.scalar_tensor_tensor(small[:, 48 + 2 * (h % 4):50 + 2 * (h % 4)], mx, -1.0, fq,
                                               ALU.mult, ALU.mult).then_inc(m_ready, 1)

            def normalised(h):
                dve.wait_ge(e_ready, 2 * h + 2)
                rs = small[:, 56 + 2 * (h % 4):58 + 2 * (h % 4)]
                own(nc.vector.reciprocal(rs, rs))
                for t, (a, b) in enumerate(((0, P), (P, 384))):
                    i = nc.vector.tensor_scalar(probs[:, h % 3, a:b], probs[:, h % 3, a:b],
                                                rs[:, t:t + 1], None, ALU.mult)
                i.then_inc(p_ready, 1)

            def head_lo(h):
                dve.wait_ge(oT_hi_ready, h + 1)
                nc.vector.tensor_tensor(oT_lo[:, h, :], scr[:, 3, 0:SEQ], oT_hi[:, h, :].bitcast(F32),
                                        ALU.subtract).then_inc(oT_ready, 1)

            for h in range(HA + 3):
                if h < HA:
                    masked(h)
                if 1 <= h < HA + 1:
                    normalised(h - 1)
                if h >= 3:
                    head_lo(h - 3)

            def update_x(stage, n, c_last, slot, n_tok, scale=None):
                for t in range(TT):
                    if t == 0:
                        dve.wait_ge(tok0_ready, n_tok + 1)
                    else:
                        dve.wait_ge(used, c_last + 1 + RING)
                    xs = x[:, t, n * NC:(n + 1) * NC]
                    if scale is None:
                        i = nc.vector.tensor_tensor(xs, acc[:, slot + t, :], xs, ALU.add)
                    else:
                        i = nc.vector.scalar_tensor_tensor(xs, acc[:, slot + t, :], nrm[:, 2, t:t + 1],
                                                           xs, ALU.mult, ALU.add)
                    i.then_inc(x_ready, 1)
                    dve.wait_ge(x_ready, 4 * stage + 2 * n + t + 1)
                    dve.sem_inc(acc_free, 1)

            for n in range(2):
                for kg in range(2):
                    split_ahead(C_WO // 4, 2 * n + kg)
                update_x(0, n, C_WO + 2 * n + 1, 2 * n, TOK_WO + n)
                if n == 1:
                    norm_lo(1, range(KD))

            def mlp(layer, norm):
                norm_factors(norm)
                with dve.Fori(0, 4) as i:
                    for s in range(4):
                        split_ahead(i + C_W1[layer] // 4, s)
                        c = i * 4 + (16 * layer + s)
                        dve.wait_ge(relu_done, c + 1)
                        dve.sem_inc(acc_free, 1)
                        dve.wait_ge(sq_ready, c + 3)
                        sq = stage_b[:, s % 2, :].rearrange("p (o t) -> p o t", o=2)
                        k = bass.ds(i * 8 + 2 * s, 2)
                        nc.vector.tensor_copy(aT_hi[:, k, :], sq).then_inc(dv.sem, 1)
                        dve.wait_ge(dv.sem, i * 4 + (dv.n + s + 1))
                        nc.vector.tensor_tensor(aT_lo[:, k, :], sq, aT_hi[:, k, :].bitcast(F32),
                                                ALU.subtract).then_inc(aT_ready, 1)
                dv.n += 16
                for n in range(2):
                    for kg in range(8):
                        if layer == 0 or n == 0 or kg < 8 - AHEAD:
                            split_ahead(C_W2[layer] // 4 + 2 * n + kg // 4, kg % 4)
                        if layer == 0 and n == 1 and kg == 2:
                            norm_lo(norm + 1, range(4))
                    update_x(1 + 2 * layer, n, C_W2[layer] + 8 * n + 7, 2 * n, TOK_W2[layer] + n, scale=2)

            mlp(0, 1)
            norm_lo(2, range(4, KD))
            norm_factors(2)

            with dve.Fori(0, 2) as i:
                for s in range(4):
                    split_ahead(i + C_QK // 4, s)
                    dve.wait_ge(used, i * 4 + (C_QK + s + 1 + RING))
                    dve.wait_ge(qk_r_ready, i * 8 + (2 * s + 2))
                    bank = acc[:, s, :]
                    nc.vector.tensor_tensor(stage_a[:, s % 2, :], bank,
                                            rope_r_sb[:, 0, :, :].rearrange("p a t -> p (a t)"), ALU.mult
                                            ).then_inc(dv.sem, 1)
                    nc.vector.tensor_tensor(stage_b[:, s % 2, :], bank,
                                            rope_r_sb[:, 1, :, :].rearrange("p a t -> p (a t)"), ALU.mult
                                            ).then_inc(t_ready, 1)
                    dve.wait_ge(t_ready, i * 4 + (s + 1))
                    dve.sem_inc(acc_free, 1)
            dv.n += 8

            def z_lo(h):
                for t in range(TT):
                    dve.wait_ge(zT_hi_ready, h * 2 + (t + 1))
                    k = bass.ds(h * 4, 4)
                    nc.vector.tensor_tensor(zT_lo[:, k, t * P:(t + 1) * P],
                                            scr[:, 3, :].rearrange("p (a t) -> p a t", t=P),
                                            zT_hi[:, k, t * P:(t + 1) * P].bitcast(F32),
                                            ALU.subtract).then_inc(zT_ready, 1)

            def head(h, first):
                for s in range(2):
                    split_ahead(h + C_VG // 4, s)
                dve.wait_ge(sr_ready, h + 1)
                nc.vector.tensor_tensor(sT[:], scr[:, 0, 0:384],
                                        decay_sb[:, bass.ds(h, 1), :].rearrange("p a t -> p (a t)"),
                                        ALU.mult).then_inc(sT_ready, 1)
                dve.wait_ge(v_r_ready, h * 2 + 2)
                dve.sem_inc(acc_free, 2)
                if not first:
                    z_lo(h - 1)
                for s in range(2, 4):
                    split_ahead(h + C_VG // 4, s)
                dve.wait_ge(sg_ready, h * 2 + 2)
                dve.sem_inc(acc_free, 2)
                dve.wait_ge(yss_ready, h * 2 + 2)
                own_r(nc.vector.tensor_tensor(small[:, 18:20], small[:, 16:18], nrm[:, 4, :], ALU.mult), h, 0)
                nc.vector.tensor_scalar(small[:, 18:20], small[:, 18:20], EPS, None,
                                        ALU.add).then_inc(var_ready, 1)
                dve.wait_ge(pow_ready, h + (npow + 1))
                own_r(nc.vector.tensor_tensor(small[:, 22:24], small[:, 20:22], nrm[:, 1, :], ALU.mult), h, 1)
                for t in range(TT):
                    nc.vector.scalar_tensor_tensor(sg[:, t, :], scr[:, 1 + t, :], small[:, 22 + t:23 + t],
                                                   sg[:, t, :], ALU.mult, ALU.mult).then_inc(z_ready, 1)

            def own_r(instruction, h, k):
                instruction.then_inc(dv.sem, 1)
                dve.wait_ge(dv.sem, h * 2 + (dv.n + k + 1))

            head(0, True)
            with dve.Fori(1, HR) as h:
                head(h, False)
            dv.n += 2 * HR
            npow += HR
            z_lo(HR - 1)

            for n in range(2):
                for kg in range(4):
                    split_ahead(C_WOUT // 4 + n, kg)
                    if n == 1 and kg == 2:
                        norm_lo(3, range(4))
                update_x(2, n, C_WOUT + 4 * n + 3, 2 * n, TOK_WOUT + n)
            norm_lo(3, range(4, KD))
            mlp(1, 3)


TOK_WO = 6
TOK_W2 = [8, 8 + 2 + 8 + 2]
TOK_VG = 10
TOK_WOUT = 18


def shape_tables():
    f = np.float32
    pos = np.arange(SEQ, dtype=f)

    def angles(width):
        h = width // 2
        inv = (f(THETA) ** (-np.arange(h, dtype=f) / f(h))).astype(f)
        a = (pos[:, None] * inv[None, :]).astype(f).astype(np.float64)
        return np.cos(a), np.sin(a)

    c, s = angles(P)
    rope_a = np.stack([np.concatenate([c, c], 1), np.concatenate([s, -s], 1)], 1)
    rope_a = np.ascontiguousarray(rope_a.reshape(TT, P, 2, P).transpose(1, 0, 2, 3).astype(f))
    c, s = angles(DK)
    rope_r = np.stack([np.stack([c.T, c.T], 1), np.stack([s.T, -s.T], 1)], 1).astype(f)
    i = np.arange(SEQ)[None, :] - np.arange(P)[:, None]
    decay = np.zeros((P, HR, 384))
    for h in range(HR):
        g = np.where(i >= 0, np.exp(np.log1p(-2.0 ** (-5.0 - h)) * np.maximum(i, 0)), 0.0)
        decay[:, h, :SEQ] = g * DK ** -0.5
        decay[:, h, SEQ:] = g[:, :P] * DK ** -0.5
    q, k = np.arange(P)[:, None], np.arange(P)[None, :]
    low = np.where(k <= q, 0.0, NEG)
    mask = np.concatenate([low, np.zeros((P, P)), low], 1)
    return [rope_a, np.ascontiguousarray(rope_r), decay.astype(f), mask.astype(f), np.eye(P, dtype=f)]


_INS = ["x", "norm_mix_g", "norm_mlp_g", "a_w_qkv", "a_q_gain", "a_k_gain", "a_w_o", "r_w_in",
        "r_w_out", "mlp_w1", "mlp_w2"]


def kernel(**inputs):
    import concourse.bacc as bacc
    from concourse.bass_utils import run_bass_kernel_spmd

    nc = bacc.Bacc("TRN2", target_bir_lowering=False, num_devices=1)
    arrays, aps = {}, {}
    named = {k: np.ascontiguousarray(inputs[k]) for k in _INS}
    for n, a in zip(("rope_a", "rope_r", "decay", "causal", "ident"), shape_tables()):
        named[n] = a
    for n, a in named.items():
        arrays[f"in_{n}"] = a
        aps[n] = nc.dram_tensor(f"in_{n}", a.shape, mybir.dt.from_np(a.dtype), kind="ExternalInput").ap()
    out = nc.dram_tensor("out_x", (1, SEQ, D), F32, kind="ExternalOutput").ap()
    tables = [aps[n] for n in ("rope_a", "rope_r", "decay", "causal", "ident")]
    program(nc, aps["x"], tables, *[aps[n] for n in _INS[1:]], out)
    return run_bass_kernel_spmd(nc, [arrays], core_ids=[0]).results[0]["out_x"]
```

```python
from contextlib import ExitStack, contextmanager

import numpy as np

import concourse.bass as bass
from concourse import mybir

F32 = mybir.dt.float32
F32R = mybir.dt.float32r
BF16 = mybir.dt.bfloat16
ACT = mybir.ActivationFunctionType
ALU = mybir.AluOpType
AX = mybir.AxisListType.X

P = 128
SEQ = 256
D = 1024
FF = 4096
TT = SEQ // P
KD = D // P
KF = FF // P
HA = 8
HR = 4
DK = D // HR
DV = 2 * D // HR
THETA = 10000.0
EPS = 1e-6
NEG = -1e30

RING = 4
AHEAD = RING - 1
CH = 2048
NC = 512
MC = 256

C_QKV = 0
C_WO = C_QKV + 12
C_W1 = [C_WO + 4, 80]
C_W2 = [C_W1[0] + 16, 96]
C_QK = C_W2[0] + 16
C_VG = C_QK + 8
C_WOUT = C_VG + 16
CHUNKS = 112
B_QKV = 0
B_WO = 12
B_W1 = [16, 64]
B_W2 = [32, 80]
B_QK = 36
B_VG = 44
B_WOUT = 60


TOK_WO = 6
TOK_VG = 10
TOK_WOUT = 18
TOK_W2 = [8, 20]

BANK_O = [3, 0]
GAIN = [0, 2, 1, 3]
WO_ORDER = [(0, 0), (1, 0), (0, 1), (1, 1)]
WOUT_ORDER = [(0, 0), (0, 1), (0, 2), (1, 0), (1, 1), (1, 2), (0, 3), (1, 3)]
QKV_ORDER = [0, 2, 1, 3, 4, 5]
SLOTS = 4 * 6 + 4


def attention_schedule():
    at = [[] for _ in range(SLOTS)]
    for k in range(0, SLOTS, 2):
        at[k].append(("split", k // 2 + AHEAD))
    for b in range(4):
        for t in range(TT):
            p = 2 * b + t
            at[4 * b + 3 + t].append(("raw", p))
            at[4 * b + 5 + t].append(("rope", p))
            at[4 * b + 7 + t].append(("T", p))
    for i in range(4):
        at[4 * (4 + i // 2) + 3 + i % 2].append(("v", i))
    for h in range(HA):
        at[S_AT[h]] += [("S", h), ("E", h)]
        at[S_AT[h] + 1].append(("N", h))
        at[P_AT[h]].append(("P", h))
        at[A_AT[h]].append(("A", h))
        if O_AT[h] is not None:
            at[O_AT[h]].append(("O", h))
    first_to_last = ["O", "split", "N", "T", "v", "raw", "A", "P", "S", "rope", "E"]
    for k in range(SLOTS):
        at[k].sort(key=lambda what: (first_to_last.index(what[0]), what[1]))
    at[SLOTS - 1] += [("O", HA - 2), ("O", HA - 1)]
    return at


S_AT = [14, 14, 16, 18, 20, 21, 23, 24]
P_AT = [16, 17, 18, 20, 23, 24, 25, 26]
A_AT = [21, 22, 22, 23, 25, 26, 27, 27]
O_AT = [21, 22, 22, 23, 26, 27, None, None]
SCHEDULE = attention_schedule()


class Ticks:

    def __init__(self, sem):
        self.sem, self.n, self.shift = sem, 0, 0

    def mark(self, instruction):
        instruction.then_inc(self.sem, 1)
        self.n += 1
        return self.n + self.shift

    def now(self):
        return self.n + self.shift


def program(nc, x_in, tables, norm_mix_g, norm_mlp_g, a_w_qkv, a_q_gain, a_k_gain, a_w_o, r_w_in,
            r_w_out, mlp_w1, mlp_w2, out):
    rope_a, rope_r, decay, causal, ident_in = tables
    with ExitStack() as ctx:
        def sb(name, shape, dt=F32):
            return ctx.enter_context(nc.sbuf_tensor(name, shape, dt))

        def sem(name):
            return ctx.enter_context(nc.semaphore(name))

        raw = sb("raw", [P, RING, CH])
        hi = sb("hi", [P, RING, CH], F32R)
        lo = sb("lo", [P, RING, CH], F32R)
        x = sb("x", [P, TT, D])
        hT_hi = sb("hT_hi", [P, KD, SEQ], F32R)
        hT_lo = sb("hT_lo", [P, KD, SEQ], F32R)
        stage_a = sb("stage_a", [P, 2, 512])
        stage_b = sb("stage_b", [P, 2, 512])
        decay_sb = sb("decay_sb", [P, HR, 384])
        pT = nc.alloc_sbuf_tensor_at("pT", [P, 4, 384], F32, offset=nc.sbuf_base - HR * 384 * 4)
        gain_rows = sb("gain_rows", [4 * KD, P])
        rope_r_sb = sb("rope_r_sb", [P, 2, 2, SEQ])
        sT = sb("sT", [P, 384])
        ident = sb("ident", [P, P])
        gcol = sb("gcol", [P, 4, KD])
        junk = sb("junk", [P, 512], BF16)
        ssq = sb("ssq", [P, TT, 2])
        nrm = sb("nrm", [P, 8, TT])
        half = sb("half", [P, 8])
        small = sb("small", [P, 64])
        sb("arena", [P, 2 * KF * SEQ])
        arena_at = nc.sbuf_base - 2 * KF * SEQ * 4

        def at(name, offset, shape, dt=F32):
            return nc.alloc_sbuf_tensor_at(name, shape, dt, offset=arena_at + offset)

        KB = 1024
        aT_hi = at("aT_hi", 0, [P, KF, SEQ], F32R)
        aT_lo = at("aT_lo", 32 * KB, [P, KF, SEQ], F32R)
        qkT = at("qkT", 0, [P, 2, HA, SEQ])
        v_att = at("v_att", 16 * KB, [P, TT, D])
        oT_hi = at("oT_hi", 24 * KB, [P, HA, SEQ], F32R)
        oT_lo = at("oT_lo", 32 * KB, [P, HA, SEQ], F32R)
        q_raw = at("q_raw", 40 * KB, [P, 2, 512])
        rot = at("rot", 44 * KB, [P, 2, 512])
        probs = at("probs", 48 * KB, [P, 3, 384])
        rope_t = at("rope_t", 61 * KB, [P, TT, 2, P])
        gains = at("gains", 63 * KB, [P, 2, P])
        rope_g = at("rope_g", 55 * KB, [P, 2, TT, 2, P])
        mask = at("mask", 59 * KB, [P, 384])
        zT_hi = at("zT_hi", 0, [P, 16, SEQ], F32R)
        zT_lo = at("zT_lo", 16 * KB, [P, 16, SEQ], F32R)
        qk_r = at("qk_r", 32 * KB, [P, 8, 2, SEQ])
        v_r = at("v_r", 48 * KB, [P, TT, DV])
        sg = at("sg", 52 * KB, [P, TT, DV])
        k_cur = at("k_cur", 56 * KB, [P, 2, SEQ])

        acc = ctx.enter_context(nc.psum_tensor("acc", [P, 4, 512], F32))
        scr = ctx.enter_context(nc.psum_tensor("scr", [P, 4, 512], F32))

        raw_ready = [sem(f"raw_ready{s}") for s in range(RING)]
        ident_in_sem = sem("ident_in")
        gains_in = sem("gains_in")
        gainsT_ready = sem("gainsT_ready")
        gcol_ready = sem("gcol_ready")
        tables_in = sem("tables_in")
        tables_r_in = sem("tables_r_in")
        x_in_ready = [sem(f"x_in_ready{n}") for n in range(2)]
        hi_ready = sem("hi_ready")
        lo_ready = sem("lo_ready")
        used = sem("used")
        tok0_ready = sem("tok0_ready")
        acc_free = sem("acc_free")
        x_ready = sem("x_ready")
        xT_ready = sem("xT_ready")
        hT_hi_ready = sem("hT_hi_ready")
        hT_ready = sem("hT_ready")
        ssq_ready = sem("ssq_ready")
        dv = Ticks(sem("dve_step"))
        pl = Ticks(sem("pool_step"))
        relu_done = sem("relu_done")
        sq_ready = sem("sq_ready")
        aT_ready = sem("aT_ready")
        var_ready = sem("var_ready")
        pow_ready = sem("pow_ready")
        r_ready = sem("r_ready")
        raw_qk = sem("raw_qk")
        u_ready = sem("u_ready")
        rot_ready = sem("rot_ready")
        rotT_ready = sem("rotT_ready")
        qkT_ready = sem("qkT_ready")
        v_ready = sem("v_ready")
        s_ready = sem("s_ready")
        m_ready = sem("m_ready")
        e_ready = sem("e_ready")
        p_ready = sem("p_ready")
        pTp_ready = sem("pTp_ready")
        pT_ready = sem("pT_ready")
        o_ready = sem("o_ready")
        oT_hi_ready = sem("oT_hi_ready")
        oT_ready = sem("oT_ready")
        t_ready = sem("t_ready")
        qk_r_ready = sem("qk_r_ready")
        k_cur_ready = sem("k_cur_ready")
        v_r_ready = sem("v_r_ready")
        sg_ready = sem("sg_ready")
        sr_ready = sem("sr_ready")
        sT_ready = sem("sT_ready")
        y_ready = sem("y_ready")
        yss_ready = sem("yss_ready")
        z_ready = sem("z_ready")
        zTp_ready = sem("zTp_ready")
        zT_hi_ready = sem("zT_hi_ready")
        zT_ready = sem("zT_ready")
        out_done = sem("out_done")

        def token_chunks(w):
            return w.rearrange("(kg kt p) (n c) -> n kg p kt c", kt=4, p=P, c=NC)

        def feature_chunks(w):
            return w.rearrange("(kt p) (m c) -> m p kt c", p=P, c=MC)

        qkv_w, wo_w, wout_w = token_chunks(a_w_qkv[0]), token_chunks(a_w_o[0]), token_chunks(r_w_out[0])
        vg_w, qk_w = token_chunks(r_w_in[0]), feature_chunks(r_w_in[0])
        w1_w = [feature_chunks(mlp_w1[i]) for i in range(2)]
        w2_w = [token_chunks(mlp_w2[i]) for i in range(2)]

        def tok_view(ring, s):
            return ring[:, s, :].rearrange("p (kt c) -> p kt c", c=NC)

        def feat_view(ring, s):
            return ring[:, s, :].rearrange("p (kt c) -> p kt c", c=MC)

        block = ctx.enter_context(nc.Block())

        @block.sync
        def _(sp):
            def load(g, s, view, src):
                sp.wait_ge(lo_ready, 4 * g + (s + 1))
                sp.dma_start(view(raw, s), src).then_inc(raw_ready[s], 16)

            def load_w1(layer):
                with sp.Fori(0, 4) as i:
                    for s in range(RING):
                        load(i + C_W1[layer] // 4, s, feat_view, w1_w[layer][i * 4 + s])

            def load_w2(layer):
                with sp.Fori(0, 2) as n:
                    for kg in range(8):
                        load(n * 2 + (C_W2[layer] // 4 + kg // 4), kg % 4, tok_view,
                             w2_w[layer][n, kg])

            xv = x_in[0].rearrange("(t p) d -> p t d", p=P)

            def load_qkv(c):
                load(c // 4, c % 4, tok_view, qkv_w[QKV_ORDER[c // 2], c % 2])

            load_qkv(0)
            for n in range(2):
                sp.dma_start(x[:, :, n * NC:(n + 1) * NC],
                             xv[:, :, n * NC:(n + 1) * NC]).then_inc(x_in_ready[n], 16)
            for c in range(1, 12):
                load_qkv(c)
            for s, (n, kg) in enumerate(WO_ORDER):
                load(C_WO // 4, s, tok_view, wo_w[n, kg])
            load_w1(0)
            load_w2(0)
            with sp.Fori(0, 2) as i:
                for s in range(RING):
                    load(i + C_QK // 4, s, feat_view, qk_w[i * 4 + s])
            with sp.Fori(0, HR) as h:
                for s in range(RING):
                    load(h + C_VG // 4, s, tok_view, vg_w[h + (4 if s < 2 else 8), s % 2])
            for c, (n, kg) in enumerate(WOUT_ORDER):
                load(C_WOUT // 4 + c // 4, c % 4, tok_view, wout_w[n, kg])
            load_w1(1)
            load_w2(1)
            ov = out[0].rearrange("(t p) d -> p t d", p=P)
            for n in range(2):
                for t in range(TT):
                    sp.wait_ge(x_ready, 4 * 3 + 2 * n + t + 1)
                    sp.dma_start(ov[:, t, n * NC:(n + 1) * NC],
                                 x[:, t, n * NC:(n + 1) * NC]).then_inc(out_done, 16)
            sp.wait_ge(out_done, 16 * 4)

        @block.gpsimd
        def _(pool):
            pool.sem_inc(sq_ready, 2)
            pool.sem_inc(qk_r_ready, 4)
            pool.dma_start(rope_t[:], rope_a).then_inc(tables_in, 16)
            for i, g in enumerate((a_q_gain, a_k_gain)):
                pool.dma_start(gains[:, i, :], g.broadcast_to([P, P])).then_inc(tables_in, 16)
            pool.dma_start(mask[:], causal).then_inc(tables_in, 16)
            pool.dma_start(rope_r_sb[:], rope_r).then_inc(tables_r_in, 16)
            half_set = pl.mark(nc.gpsimd.memset(half[:], -0.5))
            pool.wait_ge(pl.sem, half_set)
            pool.wait_ge(tables_in, 16 * 4)
            for i in range(2):
                for t in range(TT):
                    for part in range(2):
                        pl.mark(nc.gpsimd.tensor_tensor(rope_g[:, i, t, part, :], rope_t[:, t, part, :],
                                                        gains[:, i, :], ALU.mult))

            npow = 0

            def power(dst, src, n):
                nonlocal npow
                npow += 1
                pool.wait_ge(var_ready, npow)
                nc.gpsimd.tensor_tensor(dst, src, half[:, 0:n], ALU.pow).then_inc(pow_ready, 1)

            def norm_power():
                power(nrm[:, 1, :], nrm[:, 0, :], TT)

            norm_power()
            pool.wait_ge(pl.sem, pl.now())
            for p_i in range(8):
                j, t = p_i // 2, p_i % 2
                raw4 = q_raw[:, p_i % 2, :].rearrange("p (h d) -> p h d", d=P)
                cos, sin = [rope_g[:, j % 2, t, part, :].unsqueeze(1).broadcast_to([P, 4, P])
                            for part in range(2)]
                pool.wait_ge(raw_qk, 2 * p_i + 1)
                if p_i >= 2:
                    pool.wait_ge(rotT_ready, p_i - 1)
                    pool.wait_ge(rot_ready, p_i - 1)
                nc.gpsimd.tensor_tensor(rot[:, p_i % 2, :].rearrange("p (h d) -> p h d", d=P),
                                        raw4, cos, ALU.mult).then_inc(u_ready, 1)
                nc.gpsimd.tensor_tensor(stage_b[:, p_i % 2, :].rearrange("p (h d) -> p h d", d=P),
                                        raw4, sin, ALU.mult).then_inc(u_ready, 1)
                power(small[:, 8 + 4 * (p_i % 2):12 + 4 * (p_i % 2)],
                      small[:, 4 * (p_i % 2):4 * (p_i % 2) + 4], 4)
            pool.wait_ge(oT_ready, HA)
            pool.dma_start(decay_sb[:], decay).then_inc(tables_r_in, 16)

            def mlp(layer):
                norm_power()
                with pool.Fori(0, 4) as i:
                    for s in range(4):
                        c = i * 4 + (16 * layer + s)
                        pool.wait_ge(relu_done, c + 1)
                        pool.wait_ge(aT_ready, c + 1)
                        nc.gpsimd.tensor_tensor(stage_b[:, s % 2, :], stage_a[:, s % 2, :],
                                                stage_a[:, s % 2, :], ALU.mult).then_inc(sq_ready, 1)

            mlp(0)
            norm_power()
            with pool.Fori(0, 2) as i:
                for s in range(4):
                    pool.wait_ge(t_ready, i * 4 + (s + 1))
                    a = stage_a[:, s % 2, :].rearrange("p (two t) -> p two t", two=2)
                    b = stage_b[:, s % 2, :].rearrange("p (two t) -> p two t", two=2)
                    for o in range(2):
                        nc.gpsimd.tensor_tensor(qk_r[:, bass.ds(i * 4 + s, 1), o, :], a[:, o:o + 1, :],
                                                b[:, 1 - o:2 - o, :], ALU.add).then_inc(qk_r_ready, 1)
            for h in range(HR):
                power(small[:, 20:22], small[:, 18:20], TT)
            mlp(1)

        @block.tensor
        def _(pe):
            pe.sem_inc(used, RING)

            def chunk_in(g, s):
                pe.wait_ge(lo_ready, 4 * g + (s + 1 + RING))

            def three(dst, a_hi, a_lo, b_hi, b_lo, first, last):
                nc.tensor.matmul(dst, a_hi, b_hi, start=first, stop=False)
                nc.tensor.matmul(dst, a_hi, b_lo, start=False, stop=False)
                return nc.tensor.matmul(dst, a_lo, b_hi, start=False, stop=last)

            def token_chunk(c_g, s, first, last, k0, bank0, slot, lhs, after=lambda t: None):
                chunk_in(c_g, s)
                for t in range(TT):
                    if first:
                        pe.wait_ge(acc_free, bank0 + (t + 1))
                    for kt in range(4):
                        k = k0 + kt
                        m = three(acc[:, slot + t, :],
                                  lhs[0][:, k, t * P:(t + 1) * P], lhs[1][:, k, t * P:(t + 1) * P],
                                  tok_view(hi, s)[:, kt, :], tok_view(lo, s)[:, kt, :],
                                  first and kt == 0, last and kt == 3)
                    if t == 0 and last:
                        m.then_inc(tok0_ready, 1)
                    if t == 1:
                        m.then_inc(used, 1)
                    after(t)

            def token_form(g0, s0, n_chunks, bank0, slot, lhs, before=lambda kg: None,
                           between=lambda kg: None):
                for kg in range(n_chunks):
                    before(kg)
                    token_chunk(g0 + (s0 + kg) // RING, (s0 + kg) % RING, kg == 0,
                                kg == n_chunks - 1, 4 * kg, bank0, slot, lhs)
                    between(kg)

            def feature_form(g, s, bank0, hT_need=None):
                chunk_in(g, s)
                pe.wait_ge(acc_free, bank0 + 1)
                for o in range(2):
                    for kt in range(KD):
                        if hT_need is not None and o == 0:
                            pe.wait_ge(hT_ready, hT_need + kt + 1)
                        m = three(acc[:, s, o * SEQ:(o + 1) * SEQ],
                                  feat_view(hi, s)[:, kt, o * P:(o + 1) * P],
                                  feat_view(lo, s)[:, kt, o * P:(o + 1) * P],
                                  hT_hi[:, kt, :], hT_lo[:, kt, :], kt == 0, kt == KD - 1)
                m.then_inc(used, 1)

            def transpose_x(norm, kts):
                for t in range(TT):
                    for kt in kts:
                        if t == 0:
                            pe.wait_ge(hT_ready, 8 * norm + kt + 1)
                        if norm > 0:
                            pe.wait_ge(x_ready, 4 * (norm - 1) + 2 * (kt // 4) + t + 1)
                        m = nc.tensor.transpose(scr[:, kt % 4, t * P:(t + 1) * P],
                                                x[:, t, kt * P:(kt + 1) * P], ident[:])
                        if t == 1:
                            m.then_inc(xT_ready, 1)

            def early_x(norm):
                return lambda kg: transpose_x(norm, range(4)) if kg == 0 else None

            hT = (hT_hi, hT_lo)
            pe.wait_ge(ident_in_sem, 16)
            pe.wait_ge(gains_in, 32)
            nc.tensor.transpose(acc[:, 0, 0:4 * KD], gain_rows[:],
                                ident[0:4 * KD, 0:4 * KD]).then_inc(gainsT_ready, 1)
            for n in range(2):
                pe.wait_ge(x_in_ready[n], 16)
                transpose_x(0, range(4 * n, 4 * n + 4))

            def transpose_rot(p_i):
                pe.wait_ge(rot_ready, p_i + 1)
                if p_i >= 1:
                    pe.wait_ge(qkT_ready, p_i)
                for h in range(4):
                    m = nc.tensor.transpose(scr[:, 0, h * P:(h + 1) * P],
                                            rot[:, p_i % 2, h * P:(h + 1) * P], ident[:])
                m.then_inc(rotT_ready, 1)

            def scores(h):
                pe.wait_ge(qkT_ready, 4 + 4 * (h // 4))
                if h >= 1:
                    pe.wait_ge(m_ready, h)
                nc.tensor.matmul(scr[:, 2, 0:P], qkT[:, 0, h, 0:P], qkT[:, 1, h, 0:P],
                                 start=True, stop=True)
                nc.tensor.matmul(scr[:, 2, P:384], qkT[:, 0, h, P:SEQ], qkT[:, 1, h, :],
                                 start=True, stop=True).then_inc(s_ready, 1)

            def transpose_p(h):
                pe.wait_ge(p_ready, h + 1)
                if h >= 1:
                    pe.wait_ge(pT_ready, h)
                b = scr[:, 1, :]
                p = probs[:, h % 3, :]
                nc.tensor.transpose(b[:, 0:P], p[:, 0:P], ident[:])
                nc.tensor.transpose(b[:, P:2 * P], p[:, P:2 * P], ident[:])
                nc.tensor.transpose(b[:, 2 * P:384], p[:, 2 * P:384], ident[:]).then_inc(pTp_ready, 1)

            def attend(h):
                pe.wait_ge(v_ready, 2 + 2 * (h // 4))
                pe.wait_ge(pT_ready, h + 1)
                if h == 1:
                    pe.wait_ge(qkT_ready, 8)
                if h >= 2:
                    pe.wait_ge(oT_ready, h - 1)
                bank = scr[:, BANK_O[h % 2], :]
                nc.tensor.matmul(bank[:, 0:SEQ], v_att[:, 0, h * P:(h + 1) * P], pT[:, h % 4, 0:SEQ],
                                 start=True, stop=False)
                nc.tensor.matmul(bank[:, P:SEQ], v_att[:, 1, h * P:(h + 1) * P],
                                 pT[:, h % 4, SEQ:384], start=False, stop=True).then_inc(o_ready, 1)

            def behind(k):
                for what, i in SCHEDULE[k]:
                    if what == "T":
                        transpose_rot(i)
                    elif what == "S":
                        scores(i)
                    elif what == "P":
                        transpose_p(i)
                    elif what == "A":
                        attend(i)

            for c in range(12):
                if c < 2:
                    pe.wait_ge(hT_ready, 4 + 4 * (c + 1))
                token_chunk(c // 4, c % 4, c % 2 == 0, c % 2 == 1, 4 * (c % 2), B_QKV + c // 2 * 2,
                            c // 2 * 2 % 4, hT, after=lambda t: behind(2 * c + t))

            oT = (oT_hi, oT_lo)
            for s, (n, kg) in enumerate(WO_ORDER):
                pe.wait_ge(oT_ready, 4 * kg + 4)
                token_chunk(C_WO // 4, s, kg == 0, kg == 1, 4 * kg, B_WO + 2 * n, 2 * n, oT,
                            after=lambda t: behind(24 + 2 * s + t) if s < 2 else
                            transpose_x(1, range(4)) if s == 3 and t == 0 else None)
            transpose_x(1, range(4, KD))

            def mlp(layer, norm):
                feature_form(C_W1[layer] // 4, 0, B_W1[layer], hT_need=4 + 8 * norm)
                for s in range(1, 4):
                    feature_form(C_W1[layer] // 4, s, B_W1[layer] + s)
                with pe.Fori(1, 4) as i:
                    for s in range(4):
                        feature_form(i + C_W1[layer] // 4, s, i * 4 + (B_W1[layer] + s))
                for n in range(2):
                    token_form(C_W2[layer] // 4 + 2 * n, 0, 8, B_W2[layer] + 2 * n, 2 * n,
                               (aT_hi, aT_lo),
                               before=(lambda kg: pe.wait_ge(aT_ready, 2 + 16 * layer + 2 * kg + 2))
                               if n == 0 else (lambda kg: None),
                               between=early_x(norm + 1) if n == 1 and layer == 0 else (lambda kg: None))

            mlp(0, 1)
            transpose_x(2, range(4, KD))

            feature_form(C_QK // 4, 0, B_QK, hT_need=4 + 8 * 2)
            for s in range(1, 4):
                feature_form(C_QK // 4, s, B_QK + s)
            for s in range(4):
                feature_form(C_QK // 4 + 1, s, B_QK + 4 + s)

            def z_transposes(h, t):
                pe.wait_ge(z_ready, h * 2 + (t + 1))
                pe.wait_ge(zT_ready, h * 2 + (t + 1))
                for a in range(4):
                    m = nc.tensor.transpose(scr[:, 3, a * P:(a + 1) * P],
                                            sg[:, t, a * P:(a + 1) * P], ident[:])
                m.then_inc(zTp_ready, 1)

            def head(h, first):
                token_form(h + C_VG // 4, 0, 2, h * 4 + B_VG, 0, hT)
                pe.wait_ge(k_cur_ready, h + 1)
                if not first:
                    pe.wait_ge(sT_ready, h)
                for half_d in range(2):
                    nc.tensor.matmul(scr[:, 0, 0:SEQ], k_cur[:, half_d, 0:P],
                                     qk_r[:, bass.ds(h, 1), half_d, :].rearrange("p a t -> p (a t)"),
                                     start=half_d == 0, stop=half_d == 1)
                for half_d in range(2):
                    m = nc.tensor.matmul(scr[:, 0, SEQ:384], k_cur[:, half_d, P:SEQ],
                                         qk_r[:, bass.ds(h, 1), half_d, P:SEQ].rearrange("p a t -> p (a t)"),
                                         start=half_d == 0, stop=half_d == 1)
                m.then_inc(sr_ready, 1)
                if not first:
                    z_transposes(h - 1, 0)
                token_form(h + C_VG // 4, 2, 2, h * 4 + (B_VG + 2), 2, hT,
                           between=lambda kg: z_transposes(h - 1, 1) if not first and kg == 0 else None)
                pe.wait_ge(sT_ready, h + 1)
                pe.wait_ge(v_r_ready, h * 2 + 2)
                nc.tensor.matmul(scr[:, 1, :], sT[:, 0:P], v_r[:, 0, :],
                                 start=True, stop=True).then_inc(y_ready, 1)
                nc.tensor.matmul(scr[:, 2, :], sT[:, P:SEQ], v_r[:, 0, :], start=True, stop=False)
                nc.tensor.matmul(scr[:, 2, :], sT[:, SEQ:384], v_r[:, 1, :],
                                 start=False, stop=True).then_inc(y_ready, 1)

            head(0, True)
            with pe.Fori(1, HR) as h:
                head(h, False)
            for c, (n, kg) in enumerate(WOUT_ORDER):
                pe.wait_ge(zT_ready, 1 + 2 * (kg + 1))
                token_chunk(C_WOUT // 4 + c // 4, c % 4, kg == 0, kg == 3, 4 * kg, B_WOUT + 2 * n,
                            2 * n, (zT_hi, zT_lo),
                            after=lambda t: z_transposes(HR - 1, c - 1) if c in (1, 2) and t == 1 else
                            transpose_x(3, range(4)) if c == 7 and t == 0 else None)
            transpose_x(3, range(4, KD))
            mlp(1, 3)

        @block.scalar
        def _(act):
            def split(g, s):
                act.wait_ge(raw_ready[s], g * 16 + 16)
                act.wait_ge(used, 4 * g + (s + 1))
                nc.scalar.activation(hi[:, s, :], raw[:, s, :], ACT.Copy).then_inc(hi_ready, 1)

            def split_ahead(g, s):
                split(g + (s + AHEAD) // RING, (s + AHEAD) % RING)

            def norm_hi(norm, kts):
                for kt in kts:
                    act.wait_ge(xT_ready, 8 * norm + kt + 1)
                    nc.scalar.activation(hT_hi[:, kt, :], scr[:, kt % 4, 0:SEQ], ACT.Copy,
                                         scale=gcol[:, GAIN[norm], kt:kt + 1]).then_inc(hT_hi_ready, 1)

            def norm_squares(norm):
                for t in range(TT):
                    for n in range(2):
                        if norm + t + n > 0:
                            act.wait_ge(ssq_ready, 4 * norm + 2 * t + n)
                        nc.scalar.activation(junk[:], x[:, t, n * NC:(n + 1) * NC], ACT.Square,
                                             accum_out=ssq[:, t, n:n + 1]).then_inc(ssq_ready, 1)

            act.dma_start(ident[:], ident_in).then_inc(ident_in_sem, 16)
            for i, g in enumerate((norm_mix_g, norm_mlp_g)):
                act.dma_start(gain_rows[i * 2 * KD:(i + 1) * 2 * KD, :],
                              g.rearrange("l (kt p) -> (l kt) p", p=P)).then_inc(gains_in, 16)
            act.wait_ge(gainsT_ready, 1)
            nc.scalar.copy(gcol[:].rearrange("p a b -> p (a b)"), acc[:, 0, 0:4 * KD]).then_inc(gcol_ready, 1)
            split(0, 0)
            act.wait_ge(gcol_ready, 1)
            norm_hi(0, range(KD))
            split(0, 1)
            norm_squares(0)
            split(0, 2)

            def raw_copy(p_i):
                j, t = p_i // 2, p_i % 2
                if t == 0:
                    act.wait_ge(tok0_ready, j + 1)
                else:
                    act.wait_ge(used, 2 * j + 2 + RING)
                bank = acc[:, p_i % 4, :]
                if p_i >= 2:
                    act.wait_ge(rot_ready, p_i - 1)
                nc.scalar.copy(q_raw[:, p_i % 2, :], bank).then_inc(raw_qk, 1)
                nc.scalar.activation(stage_a[:, p_i % 2, :], bank, ACT.Square).then_inc(raw_qk, 1)

            def v_copy(i):
                j, t = 4 + i // 2, i % 2
                if t == 0:
                    act.wait_ge(tok0_ready, j + 1)
                else:
                    act.wait_ge(used, 2 * j + 2 + RING)
                if i == 0:
                    act.wait_ge(r_ready, 1)
                nc.scalar.activation(v_att[:, t, i // 2 * 512:(i // 2 + 1) * 512], acc[:, i, :], ACT.Copy,
                                     scale=nrm[:, 1, t:t + 1]).then_inc(v_ready, 1)

            def store_qkT(p_i):
                j, t = p_i // 2, p_i % 2
                act.wait_ge(rotT_ready, p_i + 1)
                nc.scalar.copy(qkT[:, j % 2, 4 * (j // 2):4 * (j // 2) + 4, t * P:(t + 1) * P],
                               scr[:, 0, :].rearrange("p (h t) -> p h t", t=P)
                               ).then_inc(qkT_ready, 1)

            def exponentials(h):
                act.wait_ge(m_ready, h + 1)
                for t, (a, b) in enumerate(((0, P), (P, 384))):
                    nc.scalar.activation(probs[:, h % 3, a:b], probs[:, h % 3, a:b], ACT.Exp,
                                         bias=small[:, 48 + 2 * (h % 4) + t:49 + 2 * (h % 4) + t],
                                         scale=small[:, 24 + 8 * t + h:25 + 8 * t + h],
                                         accum_out=small[:, 56 + 2 * (h % 4) + t:57 + 2 * (h % 4) + t]
                                         ).then_inc(e_ready, 1)

            def store_pT(h):
                act.wait_ge(pTp_ready, h + 1)
                if h >= 4:
                    act.wait_ge(o_ready, h - 3)
                nc.scalar.copy(pT[:, h % 4, :], scr[:, 1, 0:384]).then_inc(pT_ready, 1)

            def head_hi(h):
                act.wait_ge(o_ready, h + 1)
                nc.scalar.activation(oT_hi[:, h, :], scr[:, BANK_O[h % 2], 0:SEQ], ACT.Copy).then_inc(oT_hi_ready, 1)

            for k in range(SLOTS):
                for what, i in SCHEDULE[k]:
                    if what == "split":
                        split(i // 4, i % 4)
                    elif what == "raw":
                        raw_copy(i)
                    elif what == "T":
                        store_qkT(i)
                    elif what == "v":
                        v_copy(i)
                    elif what == "E":
                        exponentials(i)
                    elif what == "P":
                        store_pT(i)
                    elif what == "O":
                        head_hi(i)
            for s in range(2, 4):
                split_ahead(C_WO // 4, s)
            norm_hi(1, range(KD))

            def mlp(layer, norm):
                act.wait_ge(x_ready, 4 * norm)
                norm_squares(norm)
                with act.Fori(0, 4) as i:
                    for s in range(4):
                        g = i + C_W1[layer] // 4
                        split_ahead(g, s)
                        act.wait_ge(used, g * 4 + (s + 1 + RING))
                        act.wait_ge(sq_ready, i * 4 + (16 * layer + s + 1))
                        nc.scalar.activation(stage_a[:, s % 2, :], acc[:, s, :],
                                             ACT.Relu).then_inc(relu_done, 1)
                for n in range(2):
                    for kg in range(8):
                        if layer == 0 or n == 0 or kg < 8 - AHEAD:
                            split_ahead(C_W2[layer] // 4 + 2 * n + kg // 4, kg % 4)
                        if layer == 0 and n == 1 and kg == 2:
                            norm_hi(norm + 1, range(4))

            mlp(0, 1)
            norm_hi(2, range(4, KD))
            act.wait_ge(x_ready, 8)
            norm_squares(2)
            for c in range(8):
                split_ahead(C_QK // 4 + c // 4, c % 4)

            def store_zT(h, t):
                act.wait_ge(zTp_ready, h * 2 + (t + 1))
                nc.scalar.activation(zT_hi[:, bass.ds(h * 4, 4), t * P:(t + 1) * P],
                                     scr[:, 3, :].rearrange("p (a t) -> p a t", t=P),
                                     ACT.Copy).then_inc(zT_hi_ready, 1)

            def head(h, first):
                act.wait_ge(qk_r_ready, h * 2 + 14)
                if not first:
                    act.wait_ge(sr_ready, h)
                nc.scalar.copy(k_cur[:], qk_r[:, bass.ds(h + 4, 1), :, :].rearrange("p a b t -> p (a b) t")
                               ).then_inc(k_cur_ready, 1)
                for s in range(2):
                    split_ahead(h + C_VG // 4, s)
                for t in range(TT):
                    if t == 0:
                        act.wait_ge(tok0_ready, h * 2 + (TOK_VG + 1))
                    else:
                        act.wait_ge(used, h * 4 + (C_VG + 2 + RING))
                    if not first:
                        act.wait_ge(y_ready, h * 2)
                    nc.scalar.activation(v_r[:, t, :], acc[:, t, :], ACT.Copy,
                                         scale=nrm[:, 2, t:t + 1]).then_inc(v_r_ready, 1)
                if not first:
                    store_zT(h - 1, 0)
                split_ahead(h + C_VG // 4, 2)
                if not first:
                    store_zT(h - 1, 1)
                split_ahead(h + C_VG // 4, 3)
                for t in range(TT):
                    if t == 0:
                        act.wait_ge(tok0_ready, h * 2 + (TOK_VG + 2))
                    else:
                        act.wait_ge(used, h * 4 + (C_VG + 4 + RING))
                    nc.scalar.activation(sg[:, t, :], acc[:, 2 + t, :], ACT.Silu,
                                         scale=nrm[:, 1, t:t + 1]).then_inc(sg_ready, 1)
                for t in range(TT):
                    act.wait_ge(y_ready, h * 2 + (t + 1))
                    if t == 1:
                        act.wait_ge(yss_ready, h * 2 + 1)
                    elif not first:
                        act.wait_ge(z_ready, h * 2)
                    nc.scalar.activation(junk[:], scr[:, 1 + t, :], ACT.Square,
                                         accum_out=small[:, 16 + t:17 + t]).then_inc(yss_ready, 1)

            act.wait_ge(r_ready, 3)
            head(0, True)
            with act.Fori(1, HR) as h:
                head(h, False)
            for c in range(8):
                split_ahead(C_WOUT // 4 + c // 4, c % 4)
                if c in (1, 2):
                    store_zT(HR - 1, c - 1)
            norm_hi(3, range(KD))
            mlp(1, 3)

        @block.vector
        def _(dve):
            dve.sem_inc(lo_ready, RING)
            dve.sem_inc(hT_ready, 4)
            dve.sem_inc(acc_free, 4)
            dve.sem_inc(aT_ready, 2)
            dve.sem_inc(zT_ready, 1)

            def split(g, s):
                dve.wait_ge(hi_ready, 4 * g + (s + 1))
                nc.vector.tensor_tensor(lo[:, s, :], raw[:, s, :], hi[:, s, :].bitcast(F32),
                                        ALU.subtract).then_inc(lo_ready, 1)

            def split_ahead(g, s):
                split(g + (s + AHEAD) // RING, (s + AHEAD) % RING)

            def norm_lo(norm, kts):
                for kt in kts:
                    dve.wait_ge(hT_hi_ready, 8 * norm + kt + 1)
                    nc.vector.scalar_tensor_tensor(hT_lo[:, kt, :], scr[:, kt % 4, 0:SEQ],
                                                   gcol[:, GAIN[norm], kt:kt + 1],
                                                   hT_hi[:, kt, :].bitcast(F32), ALU.mult,
                                                   ALU.subtract).then_inc(hT_ready, 1)

            def own(instruction):
                dve.wait_ge(dv.sem, dv.mark(instruction))

            npow = 0

            def power_done():
                nonlocal npow
                npow += 1
                dve.wait_ge(pow_ready, npow)

            def norm_factors(norm):
                dve.wait_ge(ssq_ready, 4 * norm + 4)
                own(nc.vector.tensor_tensor(nrm[:, 0, :], ssq[:, :, 0], ssq[:, :, 1], ALU.add))
                nc.vector.tensor_scalar(nrm[:, 0, :], nrm[:, 0, :], 1.0 / D, EPS, ALU.mult,
                                        ALU.add).then_inc(var_ready, 1)
                power_done()
                own(nc.vector.tensor_tensor(nrm[:, 2, :], nrm[:, 1, :], nrm[:, 1, :], ALU.mult))
                own(nc.vector.tensor_scalar(nrm[:, 3, :], nrm[:, 2, :], 1.0 / P, None, ALU.mult))
                nc.vector.tensor_scalar(nrm[:, 4, :], nrm[:, 2, :], 1.0 / DV, None,
                                        ALU.mult).then_inc(r_ready, 1)
                dve.wait_ge(r_ready, norm + 1)

            split(0, 0)
            norm_lo(0, range(KD))
            split(0, 1)
            norm_factors(0)
            split(0, 2)

            def head_variance(p_i):
                t = p_i % 2
                ss = small[:, 4 * (p_i % 2):4 * (p_i % 2) + 4]
                dve.wait_ge(raw_qk, 2 * p_i + 2)
                dve.sem_inc(acc_free, 1)
                own(nc.vector.reduce_sum(ss, stage_a[:, p_i % 2, :].rearrange("p (h d) -> p h d", d=P),
                                         axis=AX))
                nc.vector.tensor_scalar(ss, ss, nrm[:, 3, t:t + 1], EPS, ALU.mult,
                                        ALU.add).then_inc(var_ready, 1)

            def rope(p_i):
                j, t = p_i // 2, p_i % 2
                u4 = stage_b[:, p_i % 2, :].rearrange("p (h d) -> p h d", d=P)
                r4 = rot[:, p_i % 2, :].rearrange("p (h d) -> p h d", d=P)
                pw = small[:, 8 + 4 * (p_i % 2):12 + 4 * (p_i % 2)]
                dve.wait_ge(u_ready, 2 * p_i + 2)
                for o in range(2):
                    a, b = slice(o * 64, o * 64 + 64), slice((1 - o) * 64, (1 - o) * 64 + 64)
                    dv.mark(nc.vector.tensor_tensor(r4[:, :, a], r4[:, :, a], u4[:, :, b], ALU.add))
                power_done()
                if j % 2 == 0:
                    heads = slice(24 + 8 * t + 4 * (j // 2), 28 + 8 * t + 4 * (j // 2))
                    dve.wait_ge(dv.sem, dv.now())
                    nc.vector.tensor_scalar(small[:, heads], pw, nrm[:, 1, t:t + 1],
                                            float(P) ** -0.5, ALU.mult,
                                            ALU.mult).then_inc(rot_ready, 1)
                else:
                    own(nc.vector.tensor_scalar(pw, pw, nrm[:, 1, t:t + 1], None, ALU.mult))
                    nc.vector.tensor_tensor(r4, r4, pw.unsqueeze(2).broadcast_to([P, 4, P]),
                                            ALU.mult).then_inc(rot_ready, 1)

            def v_left(i):
                dve.wait_ge(v_ready, i + 1)
                dve.sem_inc(acc_free, 1)

            def masked(h):
                dve.wait_ge(s_ready, h + 1)
                if h >= 3:
                    dve.wait_ge(pTp_ready, h - 2)
                mx = small[:, 40 + 2 * (h % 4):42 + 2 * (h % 4)]
                for t, (a, b) in enumerate(((0, P), (P, 384))):
                    dv.mark(nc.vector.tensor_tensor_reduce(
                        out=probs[:, h % 3, a:b], in0=scr[:, 2, a:b], in1=mask[:, a:b], scale=1.0,
                        scalar=-3e38, op0=ALU.add, op1=ALU.max, accum_out=mx[:, t:t + 1]))
                dve.wait_ge(dv.sem, dv.now())
                fq = small[:, 24:40].rearrange("p (t h) -> p t h", t=2)[:, :, h]
                nc.vector.scalar_tensor_tensor(small[:, 48 + 2 * (h % 4):50 + 2 * (h % 4)], mx, -1.0, fq,
                                               ALU.mult, ALU.mult).then_inc(m_ready, 1)

            def normalised(h):
                dve.wait_ge(e_ready, 2 * h + 2)
                rs = small[:, 56 + 2 * (h % 4):58 + 2 * (h % 4)]
                own(nc.vector.reciprocal(rs, rs))
                for t, (a, b) in enumerate(((0, P), (P, 384))):
                    i = nc.vector.tensor_scalar(probs[:, h % 3, a:b], probs[:, h % 3, a:b],
                                                rs[:, t:t + 1], None, ALU.mult)
                i.then_inc(p_ready, 1)

            def head_lo(h):
                dve.wait_ge(oT_hi_ready, h + 1)
                nc.vector.tensor_tensor(oT_lo[:, h, :], scr[:, BANK_O[h % 2], 0:SEQ], oT_hi[:, h, :].bitcast(F32),
                                        ALU.subtract).then_inc(oT_ready, 1)

            for k in range(SLOTS):
                for what, i in SCHEDULE[k]:
                    if what == "split":
                        split(i // 4, i % 4)
                    elif what == "raw":
                        head_variance(i)
                    elif what == "rope":
                        rope(i)
                    elif what == "v":
                        v_left(i)
                    elif what == "S":
                        masked(i)
                    elif what == "N":
                        normalised(i)
                    elif what == "O":
                        head_lo(i)

            def update_x(stage, n, c_last, slot, n_tok, scale=None, tiles=range(TT)):
                for t in tiles:
                    if t == 0:
                        dve.wait_ge(tok0_ready, n_tok + 1)
                    else:
                        dve.wait_ge(used, c_last + 1 + RING)
                    xs = x[:, t, n * NC:(n + 1) * NC]
                    if scale is None:
                        i = nc.vector.tensor_tensor(xs, acc[:, slot + t, :], xs, ALU.add)
                    else:
                        i = nc.vector.scalar_tensor_tensor(xs, acc[:, slot + t, :], nrm[:, 2, t:t + 1],
                                                           xs, ALU.mult, ALU.add)
                    i.then_inc(x_ready, 1)
                    dve.wait_ge(x_ready, 4 * stage + 2 * n + t + 1)
                    dve.sem_inc(acc_free, 1)

            split_ahead(C_WO // 4, 2)
            update_x(0, 0, C_WO + 2, 0, TOK_WO)
            split_ahead(C_WO // 4, 3)
            update_x(0, 1, C_WO + 3, 2, TOK_WO + 1, tiles=[0])
            norm_lo(1, range(4))
            update_x(0, 1, C_WO + 3, 2, TOK_WO + 1, tiles=[1])
            norm_lo(1, range(4, KD))

            def mlp(layer, norm):
                norm_factors(norm)
                with dve.Fori(0, 4) as i:
                    for s in range(4):
                        split_ahead(i + C_W1[layer] // 4, s)
                        c = i * 4 + (16 * layer + s)
                        dve.wait_ge(relu_done, c + 1)
                        dve.sem_inc(acc_free, 1)
                        dve.wait_ge(sq_ready, c + 3)
                        sq = stage_b[:, s % 2, :].rearrange("p (o t) -> p o t", o=2)
                        k = bass.ds(i * 8 + 2 * s, 2)
                        nc.vector.tensor_copy(aT_hi[:, k, :], sq).then_inc(dv.sem, 1)
                        dve.wait_ge(dv.sem, i * 4 + (dv.n + s + 1))
                        nc.vector.tensor_tensor(aT_lo[:, k, :], sq, aT_hi[:, k, :].bitcast(F32),
                                                ALU.subtract).then_inc(aT_ready, 1)
                dv.n += 16
                for n in range(2):
                    for kg in range(8):
                        if layer == 0 or n == 0 or kg < 8 - AHEAD:
                            split_ahead(C_W2[layer] // 4 + 2 * n + kg // 4, kg % 4)
                        if layer == 0 and n == 1 and kg == 2:
                            norm_lo(norm + 1, range(4))
                    update_x(1 + 2 * layer, n, C_W2[layer] + 8 * n + 7, 2 * n, TOK_W2[layer] + n, scale=2)

            mlp(0, 1)
            norm_lo(2, range(4, KD))
            norm_factors(2)

            dve.wait_ge(tables_r_in, 32)
            with dve.Fori(0, 2) as i:
                for s in range(4):
                    split_ahead(i + C_QK // 4, s)
                    dve.wait_ge(used, i * 4 + (C_QK + s + 1 + RING))
                    dve.wait_ge(qk_r_ready, i * 8 + (2 * s + 2))
                    bank = acc[:, s, :]
                    nc.vector.tensor_tensor(stage_a[:, s % 2, :], bank,
                                            rope_r_sb[:, 0, :, :].rearrange("p a t -> p (a t)"), ALU.mult
                                            ).then_inc(dv.sem, 1)
                    nc.vector.tensor_tensor(stage_b[:, s % 2, :], bank,
                                            rope_r_sb[:, 1, :, :].rearrange("p a t -> p (a t)"), ALU.mult
                                            ).then_inc(t_ready, 1)
                    dve.wait_ge(t_ready, i * 4 + (s + 1))
                    dve.sem_inc(acc_free, 1)
            dv.n += 8

            def z_lo(h, t):
                dve.wait_ge(zT_hi_ready, h * 2 + (t + 1))
                k = bass.ds(h * 4, 4)
                nc.vector.tensor_tensor(zT_lo[:, k, t * P:(t + 1) * P],
                                        scr[:, 3, :].rearrange("p (a t) -> p a t", t=P),
                                        zT_hi[:, k, t * P:(t + 1) * P].bitcast(F32),
                                        ALU.subtract).then_inc(zT_ready, 1)

            def head(h, first):
                for s in range(2):
                    split_ahead(h + C_VG // 4, s)
                dve.wait_ge(sr_ready, h + 1)
                nc.vector.tensor_tensor(sT[:], scr[:, 0, 0:384],
                                        decay_sb[:, bass.ds(h, 1), :].rearrange("p a t -> p (a t)"),
                                        ALU.mult).then_inc(sT_ready, 1)
                dve.wait_ge(v_r_ready, h * 2 + 2)
                dve.sem_inc(acc_free, 2)
                if not first:
                    z_lo(h - 1, 0)
                split_ahead(h + C_VG // 4, 2)
                if not first:
                    z_lo(h - 1, 1)
                split_ahead(h + C_VG // 4, 3)
                dve.wait_ge(sg_ready, h * 2 + 2)
                dve.sem_inc(acc_free, 2)
                dve.wait_ge(yss_ready, h * 2 + 2)
                own_r(nc.vector.tensor_tensor(small[:, 18:20], small[:, 16:18], nrm[:, 4, :], ALU.mult), h, 0)
                nc.vector.tensor_scalar(small[:, 18:20], small[:, 18:20], EPS, None,
                                        ALU.add).then_inc(var_ready, 1)
                dve.wait_ge(pow_ready, h + (npow + 1))
                own_r(nc.vector.tensor_tensor(small[:, 22:24], small[:, 20:22], nrm[:, 1, :], ALU.mult), h, 1)
                for t in range(TT):
                    nc.vector.scalar_tensor_tensor(sg[:, t, :], scr[:, 1 + t, :], small[:, 22 + t:23 + t],
                                                   sg[:, t, :], ALU.mult, ALU.mult).then_inc(z_ready, 1)

            def own_r(instruction, h, k):
                instruction.then_inc(dv.sem, 1)
                dve.wait_ge(dv.sem, h * 2 + (dv.n + k + 1))

            head(0, True)
            with dve.Fori(1, HR) as h:
                head(h, False)
            dv.n += 2 * HR
            npow += HR
            for c in range(8):
                split_ahead(C_WOUT // 4 + c // 4, c % 4)
                if c in (1, 2):
                    z_lo(HR - 1, c - 1)
                if c == 6:
                    update_x(2, 0, C_WOUT + 6, 0, TOK_WOUT)
            update_x(2, 1, C_WOUT + 7, 2, TOK_WOUT + 1, tiles=[0])
            norm_lo(3, range(4))
            update_x(2, 1, C_WOUT + 7, 2, TOK_WOUT + 1, tiles=[1])
            norm_lo(3, range(4, KD))
            mlp(1, 3)




def shape_tables():
    f = np.float32
    pos = np.arange(SEQ, dtype=f)

    def angles(width):
        h = width // 2
        inv = (f(THETA) ** (-np.arange(h, dtype=f) / f(h))).astype(f)
        a = (pos[:, None] * inv[None, :]).astype(f).astype(np.float64)
        return np.cos(a), np.sin(a)

    c, s = angles(P)
    rope_a = np.stack([np.concatenate([c, c], 1), np.concatenate([s, -s], 1)], 1)
    rope_a = np.ascontiguousarray(rope_a.reshape(TT, P, 2, P).transpose(1, 0, 2, 3).astype(f))
    c, s = angles(DK)
    rope_r = np.stack([np.stack([c.T, c.T], 1), np.stack([s.T, -s.T], 1)], 1).astype(f)
    i = np.arange(SEQ)[None, :] - np.arange(P)[:, None]
    decay = np.zeros((P, HR, 384))
    for h in range(HR):
        g = np.where(i >= 0, np.exp(np.log1p(-2.0 ** (-5.0 - h)) * np.maximum(i, 0)), 0.0)
        decay[:, h, :SEQ] = g * DK ** -0.5
        decay[:, h, SEQ:] = g[:, :P] * DK ** -0.5
    q, k = np.arange(P)[:, None], np.arange(P)[None, :]
    low = np.where(k <= q, 0.0, NEG)
    mask = np.concatenate([low, np.zeros((P, P)), low], 1)
    return [rope_a, np.ascontiguousarray(rope_r), decay.astype(f), mask.astype(f), np.eye(P, dtype=f)]


_INS = ["x", "norm_mix_g", "norm_mlp_g", "a_w_qkv", "a_q_gain", "a_k_gain", "a_w_o", "r_w_in",
        "r_w_out", "mlp_w1", "mlp_w2"]


def kernel(**inputs):
    import concourse.bacc as bacc
    from concourse.bass_utils import run_bass_kernel_spmd

    nc = bacc.Bacc("TRN2", target_bir_lowering=False, num_devices=1)
    arrays, aps = {}, {}
    named = {k: np.ascontiguousarray(inputs[k]) for k in _INS}
    for n, a in zip(("rope_a", "rope_r", "decay", "causal", "ident"), shape_tables()):
        named[n] = a
    for n, a in named.items():
        arrays[f"in_{n}"] = a
        aps[n] = nc.dram_tensor(f"in_{n}", a.shape, mybir.dt.from_np(a.dtype), kind="ExternalInput").ap()
    out = nc.dram_tensor("out_x", (1, SEQ, D), F32, kind="ExternalOutput").ap()
    tables = [aps[n] for n in ("rope_a", "rope_r", "decay", "causal", "ident")]
    program(nc, aps["x"], tables, *[aps[n] for n in _INS[1:]], out)
    return run_bass_kernel_spmd(nc, [arrays], core_ids=[0]).results[0]["out_x"]
```
